# Optimizing a Trainium2 kernel written in Bass

```python
import math
import jax
import jax.numpy as jnp
from jax import lax
import numpy as np

D_MODEL = 1024
BATCH = 1
SEQ = 256
DEPTH = 2

GRID_W = 64
CTX_LEN = 256
N_MIXERS = 4
GROUP_W = 256
CHUNK = 64
Q_BLOCK = 128
ROPE_BASE = 10000.0
MLA_HEADS = 4
MLA_NOPE = 64
MLA_ROPE = 32
MLA_V = 64
MLA_Q_LORA = 256
MLA_KV_LORA = 128
GLA_HEADS = 4
GLA_DK = 32
GLA_DV = 64
GLA_GATE_RANK = 16
GLA_GATE_NORM = 16.0
SSD_HEADS = 4
SSD_HEADDIM = 64
SSD_GROUPS = 2
SSD_STATE = 128
SSD_CONV = 3
RET_HEADS = 4
RET_DK = 32
RET_DV = 64
PEER_HEADS = 8
PEER_NKEYS = 128
PEER_EXPERTS = PEER_NKEYS * PEER_NKEYS
PEER_DKEY = 256
PEER_TOPK = 16
PEER_TOKEN_BLOCK = 128
DEEPNORM_ALPHA = (2 * DEPTH) ** 0.25
DEEPNORM_BETA = (8 * DEPTH) ** -0.25

SSD_BC = SSD_GROUPS * SSD_STATE
SSD_XBC = SSD_HEADS * SSD_HEADDIM + 2 * SSD_BC
MLA_SIZES = (MLA_Q_LORA, MLA_KV_LORA, MLA_ROPE)
GLA_SIZES = (GLA_HEADS * GLA_DK, GLA_HEADS * GLA_DK, GLA_HEADS * GLA_DV, GLA_HEADS * GLA_DV, GLA_GATE_RANK, GLA_GATE_RANK)
SSD_SIZES = (SSD_HEADS * SSD_HEADDIM, SSD_XBC, SSD_HEADS, SSD_HEADS)
RET_SIZES = (RET_HEADS * RET_DK, RET_HEADS * RET_DK, RET_HEADS * RET_DV, RET_HEADS * RET_DV)
IN_SIZES = MLA_SIZES + GLA_SIZES + SSD_SIZES + RET_SIZES
D_IN = sum(IN_SIZES)

kernel_name = 'hybrid_mla_gla_ssd_retnet_peer_dit'

F32 = jnp.float32

def layer_norm(x, g, b, eps=1e-5):
    xf = x.astype(F32)
    mu = xf.mean(-1, keepdims=True)
    xc = xf - mu
    var = jnp.mean(xc * xc, -1, keepdims=True)
    return (xc * lax.rsqrt(var + eps) * g + b).astype(x.dtype)

def rms_norm(x, g, eps=1e-6):
    xf = x.astype(F32)
    return (xf * lax.rsqrt(jnp.mean(xf * xf, -1, keepdims=True) + eps) * g).astype(x.dtype)

def head_norm(o, centre):
    of = o.astype(F32)
    if centre:
        of = of - of.mean(-1, keepdims=True)
    return (of * lax.rsqrt(jnp.mean(of * of, -1, keepdims=True) + 1e-6)).astype(o.dtype)

def modulate(x, shift, scale):
    return x * (1 + scale) + shift

def split_cols(p, sizes):
    return jnp.split(p, np.cumsum(sizes)[:-1].tolist(), axis=-1)

def partition(pieces):
    a = len(MLA_SIZES)
    b = a + len(GLA_SIZES)
    s = b + len(SSD_SIZES)
    return pieces[:a], pieces[a:b], pieces[b:s], pieces[s:]

def to_heads(t, h):
    b, l, _ = t.shape
    return t.reshape(b, l, h, -1).transpose(0, 2, 1, 3)

def merge_heads(t):
    b, h, l, d = t.shape
    return t.transpose(0, 2, 1, 3).reshape(b, l, h * d)

def rope_tables(pos, dim):
    half = dim // 2
    freqs = ROPE_BASE ** (-jnp.arange(half, dtype=F32) / half)
    ang = pos.astype(F32)[:, None] * freqs
    return jnp.cos(ang), jnp.sin(ang)

def rotate(x, tab):
    cos, sin = tab
    cos = cos.astype(x.dtype)
    sin = sin.astype(x.dtype)
    h = x.shape[-1] // 2
    x1, x2 = x[..., :h], x[..., h:]
    return jnp.concatenate([x1 * cos - x2 * sin, x1 * sin + x2 * cos], -1)

def axial_rope(x, axial):
    h = x.shape[-1] // 2
    return jnp.concatenate([rotate(x[..., :h], axial[0]), rotate(x[..., h:], axial[1])], -1)

def attention(q, k, v):
    s = jnp.einsum('bhqd,bhkd->bhqk', q, k).astype(F32) * (q.shape[-1] ** -0.5)
    return jnp.einsum('bhqk,bhkv->bhqv', jax.nn.softmax(s, axis=-1).astype(v.dtype), v)

def blocked_attention(q, k, v):
    b, h, l, d = q.shape
    nb = l // Q_BLOCK
    qb = q.reshape(b, h, nb, Q_BLOCK, d).transpose(2, 0, 1, 3, 4)
    ob = lax.map(lambda qq: attention(qq, k, v), qb)
    return ob.transpose(1, 2, 0, 3, 4).reshape(b, h, l, -1)

def chunk_scan(q, k, v, lg, s0):
    b, h, l, _ = k.shape
    n = l // CHUNK
    dt = v.dtype
    mask = jnp.tril(jnp.ones((CHUNK, CHUNK), bool))[:, :, None]

    def chunks(t):
        return t.reshape(b, h, n, CHUNK, t.shape[-1]).transpose(2, 0, 1, 3, 4)

    def step(s, inp):
        qc, kc, vc, gc = inp
        cum = jnp.cumsum(gc.astype(F32), axis=2)
        last = cum[:, :, -1:]
        inter = jnp.einsum('bhik,bhkv->bhiv', qc * jnp.exp(cum).astype(dt), s)
        decay = jnp.exp(jnp.where(mask, cum[:, :, :, None] - cum[:, :, None], -jnp.inf)).astype(dt)
        if gc.shape[-1] == 1:
            att = jnp.einsum('bhik,bhjk->bhij', qc, kc) * decay[..., 0]
        else:
            att = jnp.einsum('bhik,bhjk,bhijk->bhij', qc, kc, decay)
        o = inter + jnp.einsum('bhij,bhjv->bhiv', att, vc)
        s = jnp.exp(last[:, :, 0])[..., None].astype(dt) * s + jnp.einsum('bhjk,bhjv->bhkv', kc * jnp.exp(last - cum).astype(dt), vc)
        return s, o

    s_fin, o = lax.scan(step, s0, (chunks(q), chunks(k), chunks(v), chunks(lg)))
    return o.transpose(1, 2, 0, 3, 4).reshape(b, h, l, -1), s_fin

def final_state(k, v, lg):
    cum = jnp.cumsum(lg.astype(F32), axis=2)
    return jnp.einsum('bhjk,bhjv->bhkv', k * jnp.exp(cum[:, :, -1:] - cum).astype(v.dtype), v)

def bidir_scan(lat_dirs, ctx_dirs, need_ctx):
    out_lat, out_ctx = [], []
    for d, (lat, ctxd) in enumerate(zip(lat_dirs, ctx_dirs)):
        flip = (lambda t: jnp.flip(t, axis=2)) if d == 1 else (lambda t: t)
        qc, kc, vc, gc = (None if t is None else flip(t) for t in ctxd)
        if need_ctx:
            s0 = jnp.zeros(kc.shape[:2] + (kc.shape[-1], vc.shape[-1]), vc.dtype)
            oc, state = chunk_scan(qc, kc, vc, gc, s0)
            out_ctx.append(flip(oc))
        else:
            state = final_state(kc, vc, gc)
        ql, kl, vl, gl = (flip(t) for t in lat)
        ol, _ = chunk_scan(ql, kl, vl, gl, state)
        out_lat.append(flip(ol))
    return out_lat[0] + out_lat[1], (out_ctx[0] + out_ctx[1] if need_ctx else None)

def mla_q(c_q, g_q, w_uq, axial):
    q = to_heads(rms_norm(c_q, g_q) @ w_uq, MLA_HEADS)
    if axial is None:
        return q
    return jnp.concatenate([q[..., :MLA_NOPE], axial_rope(q[..., MLA_NOPE:], axial)], -1)

def mla_kv(c_kv, k_rope, g_kv, w_uk, w_uv, axial):
    kv = rms_norm(c_kv, g_kv)
    k_nope = to_heads(kv @ w_uk, MLA_HEADS)
    v = to_heads(kv @ w_uv, MLA_HEADS)
    if axial is not None:
        k_rope = axial_rope(k_rope, axial)
    k_rope = jnp.broadcast_to(k_rope[:, None], k_nope.shape[:3] + (MLA_ROPE,))
    return jnp.concatenate([k_nope, k_rope], -1), v

def mla_mixer(pl, pc, g_q, w_uq, g_kv, w_uk, w_uv, axial, need_ctx):
    cq_l, ckv_l, kr_l = pl
    cq_c, ckv_c, kr_c = pc
    k_c, v_c = mla_kv(ckv_c, kr_c, g_kv, w_uk, w_uv, None)
    k_l, v_l = mla_kv(ckv_l, kr_l, g_kv, w_uk, w_uv, axial)
    q_l = mla_q(cq_l, g_q, w_uq, axial)
    o_l = blocked_attention(q_l, jnp.concatenate([k_c, k_l], 2), jnp.concatenate([v_c, v_l], 2))
    o_c = merge_heads(attention(mla_q(cq_c, g_q, w_uq, None), k_c, v_c)) if need_ctx else None
    return merge_heads(o_l), o_c

def gla_prep(p, w_gf, b_gf, w_gb, b_gb, with_q):
    q, k, v, r, lr_f, lr_b = p
    q = (to_heads(q, GLA_HEADS) * GLA_DK ** -0.5) if with_q else None
    k = to_heads(k, GLA_HEADS)
    v = to_heads(v, GLA_HEADS)

    def log_gate(lr, w, b):
        return to_heads(jax.nn.log_sigmoid((lr @ w + b).astype(F32)) / GLA_GATE_NORM, GLA_HEADS)

    return (q, k, v, log_gate(lr_f, w_gf, b_gf)), (q, k, v, log_gate(lr_b, w_gb, b_gb)), r

def gla_mixer(pl, pc, w_gf, b_gf, w_gb, b_gb, g_out, need_ctx):
    lat_f, lat_b, r_l = gla_prep(pl, w_gf, b_gf, w_gb, b_gb, True)
    ctx_f, ctx_b, r_c = gla_prep(pc, w_gf, b_gf, w_gb, b_gb, need_ctx)
    o_l, o_c = bidir_scan((lat_f, lat_b), (ctx_f, ctx_b), need_ctx)

    def out(o, r):
        return merge_heads(head_norm(o, False)) * g_out * jax.nn.silu(r)

    return out(o_l, r_l), (out(o_c, r_c) if need_ctx else None)

def depthwise_conv(x, w, b):
    pad = w.shape[0] // 2
    y = lax.conv_general_dilated(x, w[:, None, :], (1,), [(pad, pad)],
                                 dimension_numbers=('NWC', 'WIO', 'NWC'), feature_group_count=x.shape[-1])
    return y + b

def ssd_prep(p, conv_w, conv_b, dtb_f, dtb_b, alog_f, alog_b, with_q):
    z, xbc, dt_f, dt_b = p
    xbc = jax.nn.silu(depthwise_conv(xbc, conv_w, conv_b))
    xs, bm, cm = split_cols(xbc, (SSD_HEADS * SSD_HEADDIM, SSD_BC, SSD_BC))
    rep = SSD_HEADS // SSD_GROUPS
    xh = to_heads(xs, SSD_HEADS)
    bh = jnp.repeat(to_heads(bm, SSD_GROUPS), rep, axis=1)
    ch = jnp.repeat(to_heads(cm, SSD_GROUPS), rep, axis=1) if with_q else None

    def direction(dt_raw, dt_bias, a_log):
        dt = jax.nn.softplus(dt_raw.astype(F32) + dt_bias).transpose(0, 2, 1)[..., None]
        la = dt * -jnp.exp(a_log.astype(F32))[:, None, None]
        return (ch, bh * dt.astype(bh.dtype), xh, la)

    return direction(dt_f, dtb_f, alog_f), direction(dt_b, dtb_b, alog_b), xh, z

def ssd_mixer(pl, pc, conv_w, conv_b, dtb_f, dtb_b, alog_f, alog_b, d_skip, g_out, need_ctx):
    lat_f, lat_b, x_l, z_l = ssd_prep(pl, conv_w, conv_b, dtb_f, dtb_b, alog_f, alog_b, True)
    ctx_f, ctx_b, x_c, z_c = ssd_prep(pc, conv_w, conv_b, dtb_f, dtb_b, alog_f, alog_b, need_ctx)
    o_l, o_c = bidir_scan((lat_f, lat_b), (ctx_f, ctx_b), need_ctx)

    def out(o, xh, z):
        y = merge_heads(o + d_skip[:, None, None] * xh)
        return rms_norm(y * jax.nn.silu(z), g_out)

    return out(o_l, x_l, z_l), (out(o_c, x_c, z_c) if need_ctx else None)

def ret_log_decay():
    return jnp.log1p(-jnp.exp2(-5.0 - jnp.arange(RET_HEADS, dtype=F32)))

def ret_prep(p, rope, with_q):
    q, k, v, g = p
    q = to_heads(q, RET_HEADS) if with_q else None
    k = to_heads(k, RET_HEADS) * RET_DK ** -0.5
    if rope is not None:
        q = rotate(q, rope)
        k = rotate(k, rope)
    v = to_heads(v, RET_HEADS)
    la = jnp.broadcast_to(ret_log_decay()[:, None, None], (k.shape[0], RET_HEADS, k.shape[2], 1))
    d = (q, k, v, la)
    return (d, d), g

def ret_mixer(pl, pc, rope, need_ctx):
    lat, g_l = ret_prep(pl, rope, True)
    ctx_d, g_c = ret_prep(pc, None, need_ctx)
    o_l, o_c = bidir_scan(lat, ctx_d, need_ctx)

    def out(o, g):
        return merge_heads(head_norm(o, True)) * jax.nn.silu(g)

    return out(o_l, g_l), (out(o_c, g_c) if need_ctx else None)

def peer(x, w_q, sub_keys, u_tab, v_tab):
    b, l, d = x.shape
    t = x.reshape(-1, d)
    nb = t.shape[0] // PEER_TOKEN_BLOCK
    half = PEER_DKEY // 2

    def block(xb):
        q = (xb @ w_q).reshape(xb.shape[0], PEER_HEADS, PEER_DKEY)
        s1 = jnp.einsum('thd,kd->thk', q[..., :half], sub_keys[0]).astype(F32)
        s2 = jnp.einsum('thd,kd->thk', q[..., half:], sub_keys[1]).astype(F32)
        v1, i1 = lax.top_k(s1, PEER_TOPK)
        v2, i2 = lax.top_k(s2, PEER_TOPK)
        cand = (v1[..., :, None] + v2[..., None, :]).reshape(xb.shape[0], PEER_HEADS, PEER_TOPK * PEER_TOPK)
        vs, ci = lax.top_k(cand, PEER_TOPK)
        e = (jnp.take_along_axis(i1, ci // PEER_TOPK, -1) * PEER_NKEYS
             + jnp.take_along_axis(i2, ci % PEER_TOPK, -1))
        gate = jax.nn.softmax(vs, axis=-1).astype(xb.dtype)
        u = jnp.take(u_tab, e, axis=0)
        vv = jnp.take(v_tab, e, axis=0)
        act = jax.nn.gelu(jnp.einsum('td,thkd->thk', xb, u), approximate=False) * gate
        return jnp.einsum('thk,thkd->td', act, vv)

    out = lax.map(block, t.reshape(nb, PEER_TOKEN_BLOCK, d))
    return out.reshape(b, l, d)

def setup_inputs(seed: int = 0) -> dict:
    key = jax.random.key(seed)
    ks = iter(jax.random.split(key, 40))

    def nrm(shape, scale):
        return jax.random.normal(next(ks), shape, F32) * scale

    def gain(shape):
        return 1.0 + nrm(shape, 0.02)

    def dt_bias():
        dt = jnp.exp(jax.random.uniform(next(ks), (DEPTH, SSD_HEADS), F32) * (math.log(0.1) - math.log(0.001)) + math.log(0.001))
        return dt + jnp.log(-jnp.expm1(-dt))

    def a_log():
        return jnp.log(jax.random.uniform(next(ks), (DEPTH, SSD_HEADS), F32, 1.0, 16.0))

    L = DEPTH
    D = D_MODEL
    D_MIX = N_MIXERS * GROUP_W
    return {
        'x': nrm((BATCH, SEQ, D), 1.0),
        'c': nrm((BATCH, D), 1.0),
        'ctx': nrm((BATCH, CTX_LEN, D), 1.0),
        'c_ctx': nrm((D,), 1.0),
        'w_ada': nrm((L, D, 6 * D), D ** -0.5),
        'b_ada': nrm((L, 6 * D), 0.02),
        'w_in': nrm((L, D, D_IN), D ** -0.5),
        'mla_g_q': gain((L, MLA_Q_LORA)),
        'mla_w_uq': nrm((L, MLA_Q_LORA, MLA_HEADS * (MLA_NOPE + MLA_ROPE)), MLA_Q_LORA ** -0.5),
        'mla_g_kv': gain((L, MLA_KV_LORA)),
        'mla_w_uk': nrm((L, MLA_KV_LORA, MLA_HEADS * MLA_NOPE), MLA_KV_LORA ** -0.5),
        'mla_w_uv': nrm((L, MLA_KV_LORA, MLA_HEADS * MLA_V), MLA_KV_LORA ** -0.5),
        'gla_w_gf': nrm((L, GLA_GATE_RANK, GLA_HEADS * GLA_DK), GLA_GATE_RANK ** -0.5),
        'gla_b_gf': nrm((L, GLA_HEADS * GLA_DK), 0.02),
        'gla_w_gb': nrm((L, GLA_GATE_RANK, GLA_HEADS * GLA_DK), GLA_GATE_RANK ** -0.5),
        'gla_b_gb': nrm((L, GLA_HEADS * GLA_DK), 0.02),
        'gla_g': gain((L, GLA_HEADS * GLA_DV)),
        'ssd_conv_w': nrm((L, SSD_CONV, SSD_XBC), SSD_CONV ** -0.5),
        'ssd_conv_b': nrm((L, SSD_XBC), 0.02),
        'ssd_dt_bias_f': dt_bias(),
        'ssd_dt_bias_b': dt_bias(),
        'ssd_a_log_f': a_log(),
        'ssd_a_log_b': a_log(),
        'ssd_d': gain((L, SSD_HEADS)),
        'ssd_g': gain((L, SSD_HEADS * SSD_HEADDIM)),
        'w_out': nrm((L, D_MIX, D), DEEPNORM_BETA * D_MIX ** -0.5),
        'ln1_g': gain((L, D)),
        'ln1_b': nrm((L, D), 0.02),
        'peer_w_q': nrm((L, D, PEER_HEADS * PEER_DKEY), D ** -0.5),
        'peer_keys': nrm((L, 2, PEER_NKEYS, PEER_DKEY // 2), (PEER_DKEY // 2) ** -0.5),
        'peer_u': nrm((L, PEER_EXPERTS, D), D ** -0.5),
        'peer_v': nrm((L, PEER_EXPERTS, D), DEEPNORM_BETA * PEER_HEADS ** -0.5),
        'ln2_g': gain((L, D)),
        'ln2_b': nrm((L, D), 0.02),
    }

def reference(x, c, ctx, c_ctx, w_ada, b_ada, w_in, mla_g_q, mla_w_uq, mla_g_kv, mla_w_uk, mla_w_uv,
              gla_w_gf, gla_b_gf, gla_w_gb, gla_b_gb, gla_g, ssd_conv_w, ssd_conv_b, ssd_dt_bias_f,
              ssd_dt_bias_b, ssd_a_log_f, ssd_a_log_b, ssd_d, ssd_g, w_out, ln1_g, ln1_b, peer_w_q,
              peer_keys, peer_u, peer_v, ln2_g, ln2_b):
    seq = x.shape[1]
    rows = seq // GRID_W
    row = jnp.repeat(jnp.arange(rows), GRID_W)
    col = jnp.tile(jnp.arange(GRID_W), rows)
    axial = (rope_tables(row, MLA_ROPE // 2), rope_tables(col, MLA_ROPE // 2))
    ret_rope = rope_tables(jnp.arange(seq), RET_DK)
    s_lat = jax.nn.silu(c)
    s_ctx = jax.nn.silu(c_ctx)
    xc = ctx
    for i in range(DEPTH):
        need_ctx = i < DEPTH - 1
        mod = [t[:, None, :] for t in jnp.split(s_lat @ w_ada[i] + b_ada[i], 6, axis=-1)]
        mod_c = jnp.split(s_ctx @ w_ada[i] + b_ada[i], 6, axis=-1)
        p_mla, p_gla, p_ssd, p_ret = partition(split_cols(modulate(x, mod[0], mod[1]) @ w_in[i], IN_SIZES))
        c_mla, c_gla, c_ssd, c_ret = partition(split_cols(modulate(xc, mod_c[0], mod_c[1]) @ w_in[i], IN_SIZES))
        outs = (
            mla_mixer(p_mla, c_mla, mla_g_q[i], mla_w_uq[i], mla_g_kv[i], mla_w_uk[i], mla_w_uv[i], axial, need_ctx),
            gla_mixer(p_gla, c_gla, gla_w_gf[i], gla_b_gf[i], gla_w_gb[i], gla_b_gb[i], gla_g[i], need_ctx),
            ssd_mixer(p_ssd, c_ssd, ssd_conv_w[i], ssd_conv_b[i], ssd_dt_bias_f[i], ssd_dt_bias_b[i],
                      ssd_a_log_f[i], ssd_a_log_b[i], ssd_d[i], ssd_g[i], need_ctx),
            ret_mixer(p_ret, c_ret, ret_rope, need_ctx),
        )
        y = jnp.concatenate([o[0] for o in outs], -1) @ w_out[i]
        x = layer_norm(DEEPNORM_ALPHA * x + mod[2] * y, ln1_g[i], ln1_b[i])
        f = peer(modulate(x, mod[3], mod[4]), peer_w_q[i], peer_keys[i], peer_u[i], peer_v[i])
        x = layer_norm(DEEPNORM_ALPHA * x + mod[5] * f, ln2_g[i], ln2_b[i])
        if need_ctx:
            yc = jnp.concatenate([o[1] for o in outs], -1) @ w_out[i]
            xc = layer_norm(DEEPNORM_ALPHA * xc + mod_c[2] * yc, ln1_g[i], ln1_b[i])
            fc = peer(modulate(xc, mod_c[3], mod_c[4]), peer_w_q[i], peer_keys[i], peer_u[i], peer_v[i])
            xc = layer_norm(DEEPNORM_ALPHA * xc + mod_c[5] * fc, ln2_g[i], ln2_b[i])
    return x


_drawn_inputs = setup_inputs


def setup_inputs(seed=0):
    import zlib

    import numpy as np

    out = dict(_drawn_inputs(seed))
    spreads = {}
    factors = {'b_ada': 2.939,
     'mla_g_q': 8.0,
     'mla_g_kv': 8.0,
     'mla_w_uk': 2.688,
     'gla_b_gf': 8.0,
     'gla_b_gb': 8.0,
     'gla_g': 8.0,
     'ssd_conv_b': 8.0,
     'ssd_a_log_f': 4.205,
     'ssd_d': 8.0,
     'ssd_g': 8.0}
    for name, (base, spread) in spreads.items():
        noise = np.random.default_rng([zlib.crc32(name.encode()), seed]).standard_normal(out[name].shape)
        drawn = base * np.exp(spread * noise) if base else spread * noise
        out[name] = jnp.asarray(drawn.astype(out[name].dtype))
    for name, factor in factors.items():
        out[name] = (out[name] * factor).astype(out[name].dtype)
    return out
```

```python
from contextlib import ExitStack

import concourse.bass as bass
import numpy as np
from concourse import mybir

F32 = mybir.dt.float32
U32 = mybir.dt.uint32
ALU = mybir.AluOpType
ACT = mybir.ActivationFunctionType
AX = mybir.AxisListType

P = 128
D = 1024
KD = D // P
DEPTH = 2
CTX = 256
SEQ = 256
TOK = CTX + SEQ
NT = TOK // P
GRID_W = 64
HEADS = 4
QLORA, KVLORA, NOPE, ROPE, VD = 256, 128, 64, 32, 64
QKD = NOPE + ROPE
DK, DV = 32, 64
RANK = 16
STATE = 128
GW = HEADS * DV
XBC = 768
NXB = XBC // P
ALPHA = (2 * DEPTH) ** 0.25
PH, NKEY, TOPK = 8, 128, 16
HALF = 128
CHUNK = 4096

O_CQ, O_CKV, O_KR = 0, 256, 384
O_GQ, O_GK, O_GV, O_GR, O_GL = 416, 544, 672, 928, 1184
O_Z, O_DT = 1216, 1472
O_RQ, O_RK, O_RV, O_RG = 1480, 1608, 1736, 1992
NPT = 2248
NWIN = 6
NWOUT = 2
NWQ = 4
NADA = 12
PAIRS = 64

CONST = {}
_at = 0
for _name, _n in (("maskF", P), ("maskB", P), ("negF", P), ("negB", P), ("retD", HEADS * P), ("retQF", P), ("retQB", P),
                  ("blockdiag", GW), ("headmask", HEADS), ("retWF", HEADS), ("retWB", HEADS), ("retDec", 1),
                  ("ones", P), ("cosA", NT * ROPE), ("sinA", NT * ROPE), ("cosR", NT * DK), ("sinR", NT * DK)):
    CONST[_name] = (_at, _n)
    _at += _n
NCONST = _at
NSW = 2 * HEADS * QKD + 2 * GW + 2 * P
C_GQ, C_GKV, C_BGF, C_BGB, C_CW, C_CB = 0, 2, 3, 4, 5, 5 + 3 * NXB
NCOL = C_CB + NXB
R_GLA, R_SSD, R_DTB, R_ALOG, R_DSK = 0, GW, 2 * GW, 2 * GW + 8, 2 * GW + 16
NROW = R_DSK + 4


def build(nc, A, out):
    ctx = ExitStack()
    with ctx:
        def sb(name, shape, dt=F32):
            return ctx.enter_context(nc.sbuf_tensor(name, shape, dt))

        sems = {}

        def S(name):
            if name not in sems:
                sems[name] = ctx.enter_context(nc.semaphore(name))
            return sems[name]

        X = sb("X", [P, NT, D])
        arena = sb("arena", [P, 32768])
        stream = sb("stream", [P, 2, CHUNK])
        xT = sb("xT", [P, KD * 256])
        rows3 = sb("rows3", [P, 3 * D])
        actv = sb("actv", [P, 4, 256])
        picks = sb("picks", [P, 3, 256])
        ident = sb("ident", [P, P])
        iota = sb("iota", [P, P])
        modc = sb("modc", [P, 2, 6, KD])
        keysT = sb("keysT", [P, 2, NKEY])
        small = sb("small", [P, 160])
        bank = [ctx.enter_context(nc.psum_tensor(f"bank{i}", [P, 512], F32)) for i in range(8)]
        modd = nc.dram_tensor("modd", (2, DEPTH, 6 * D), F32, kind="Internal").ap()

        def region(base, n, tensor=arena):
            return tensor[:, base:base + n]

        a0 = 0
        place = {}
        for name, n in (("xm", KD * TOK), ("pt", NT * NPT), ("xb", NXB * TOK), ("cv", NXB * TOK), ("con", NCONST),
                        ("sw", NSW), ("col", NCOL), ("row", NROW), ("ln", 4 * D)):
            place[name] = a0
            a0 += n
        W2 = a0
        assert 32768 - W2 >= 4608, W2
        XM = place["xm"]
        xmT = region(XM, KD * TOK).rearrange("p (k t) -> p k t", k=KD)
        ptok = region(place["pt"], NT * NPT).rearrange("p (t n) -> p t n", t=NT)
        xbT = region(place["xb"], NXB * TOK).rearrange("p (b t) -> p b t", b=NXB)
        xBtok = region(place["xb"], NT * 512).rearrange("p (t n) -> p t n", t=NT)
        cvT = region(place["cv"], NXB * TOK).rearrange("p (b t) -> p b t", b=NXB)
        con = region(place["con"], NCONST)
        sw = region(place["sw"], NSW)
        wuq = sw[:, 0:768].rearrange("p (k n) -> p k n", k=2)
        wuk, wuv = sw[:, 768:1024], sw[:, 1024:1280]
        wg = sw[0:32, 1280:1536].rearrange("p (d n) -> p d n", d=2)
        col = region(place["col"], NCOL)
        row = region(place["row"], NROW)
        lnr = region(place["ln"], 4 * D).rearrange("p (r n) -> p r n", r=4)

        def C(name):
            a, n = CONST[name]
            return con[:, a:a + n]

        def scratch(base, n, tensor=arena, parts=P):
            return tensor[0:parts, base:base + n]

        def split(ap, **kw):
            names = " ".join(kw)
            return ap.rearrange(f"p ({names}) -> p {names}", **{k: v for k, v in kw.items()})

        def spread(ap, shape, axis):
            return ap.unsqueeze(axis).to_broadcast(shape)

        cqT = split(scratch(XM, 1024), k=2, t=TOK)
        ckvT = scratch(XM + 1024, 512)
        vtok = split(scratch(XM + 1536, 1024), t=NT, n=GW)
        probs = split(scratch(XM + 2560, 1024), s=2, n=512)
        qtok = split(scratch(0, 1536, rows3), t=NT, h=HEADS, n=QKD)
        ktok = split(scratch(1536, 1536, rows3), t=NT, h=HEADS, n=QKD)
        qT = split(scratch(W2, 2048), h=HEADS, t=TOK)
        kT = split(scratch(W2 + 2048, 2048), h=HEADS, t=TOK)
        pT = split(scratch(0, 1024, xT), s=2, n=512)
        ropeA = split(scratch(1024, 512, xT), t=NT, h=HEADS, n=ROPE)
        ropeB = split(scratch(1536, 512, xT), t=NT, h=HEADS, n=ROPE)
        gz = scratch(XM, 1024)
        ge = scratch(XM + 1024, 1024)
        gc = scratch(XM + 2048, 1024)
        lrT = scratch(XM + 3072, 512)
        gqT = scratch(XM + 3584, 512)
        gkT = scratch(W2, 512)
        gE1 = scratch(W2 + 512, 1024)
        gE2 = scratch(W2 + 1536, 1024)
        gKtok = split(scratch(W2 + 2560, 1024), d=2, t=NT, n=P)
        gQx = split(scratch(W2 + 3584, 1024), d=2, h=HEADS, i=P)
        states = split(scratch(0, 2048, xT), d=2, t=NT, n=GW)
        mats = split(scratch(0, 2048, rows3), s=2, d=2, n=512)
        work = split(scratch(2048, 1024, rows3), s=4, n=GW)
        rA = split(scratch(XM, 1024), t=NT, h=8, n=DK)
        rB = split(scratch(XM + 1024, 1024), t=NT, h=8, n=DK)
        rqT = split(scratch(XM + 2048, 512), t=NT, n=P)
        rkT = split(scratch(XM + 2560, 512), t=NT, n=P)
        rQ = split(scratch(XM + 3072, 1024), d=2, t=NT, n=P)
        rV = split(scratch(W2, 2048), d=2, t=NT, n=GW)
        rQx = split(scratch(W2 + 2048, 1024), s=2, h=HEADS, i=P)
        sm = scratch(XM, 512)
        s_dt, s_la, s_cum, s_w, s_el, s_t = (split(sm[:, 32 * i:32 * i + 32], t=NT, n=8) for i in range(6))
        laM = split(scratch(XM + 512, 1024), d=2, h=HEADS, i=P)
        sD = split(scratch(XM + 1536, 1024), d=2, h=HEADS, i=P)
        sE = split(scratch(XM + 2560, 1024), d=2, h=HEADS, i=P)
        sQ = split(scratch(W2, 1024), d=2, h=HEADS, i=P)
        sV = split(scratch(W2 + 1024, 2048), d=2, t=NT, n=GW)
        sM = split(scratch(W2 + 3072, 1024), d=2, n=512)
        sVw = split(scratch(0, 2048, rows3), d=2, t=NT, n=GW)
        norm_sq = split(scratch(XM, 1024), t=NT, n=GW)
        vals = split(scratch(0, 512), t=2, b=16, n=16)
        idxu = split(scratch(512, 512).bitcast(U32), t=2, b=16, n=16)
        idxf = split(scratch(1024, 512), t=2, b=16, n=16)
        cand = split(scratch(1536, 2048), h=PH, n=256)
        ctmp = scratch(3584, 256)
        vsel = split(scratch(3840, 256), t=2, h=PH, n=16)
        cidx = scratch(4096, 256).bitcast(U32)
        cidxu = split(cidx, t=2, h=PH, n=16)
        cab = scratch(4352, 512).bitcast(U32)
        cabf = scratch(4864, 512)
        eq = split(scratch(5376, 2048), h=PH, k=16, a=16)
        sel = split(scratch(7424, 768), w=3, t=2, n=P)
        gates = split(scratch(0, 32768), t=256, i=P)
        hotJ = split(scratch(0, 1024, rows3), s=2, u=4, n=P)
        hotI = split(scratch(1024, 1024, rows3), s=2, u=4, n=P)
        grow = split(scratch(0, 3072, rows3), r=3, n=D)
        xTk = split(xT[:, :], k=KD, t=256)

        class Count:

            def __init__(self, eng, own):
                self.eng, self.own, self.n = eng, own, {}

            def up(self, name, n=1):
                self.n[name] = self.n.get(name, 0) + n
                return self.n[name]

            def step(self, ins):
                ins.then_inc(S(self.own), 1)
                self.eng.wait_ge(S(self.own), self.up(self.own))

            def tell(self, name):
                self.eng.sem_inc(S(name), 1)
                self.up(name)

            def await_(self, name, n=1):
                self.eng.wait_ge(S(name), self.up(name, n))

        class Filler:

            def __init__(self, who, first):
                self.who, self.first, self.n = who, first, 0

            def open(self, pe):
                if self.n >= 4:
                    pe.wait_ge(S(f"{self.who}_emptied"), self.n - 3)
                self.n += 1
                return bank[self.first + (self.n - 1) % 4]

            def close(self, ins):
                ins.then_inc(S(f"{self.who}_filled"), 1)

            def flushed(self, pe):
                pe.wait_ge(S(f"{self.who}_filled"), self.n)

            def settled(self, pe):
                if self.n:
                    pe.wait_ge(S(f"{self.who}_emptied"), self.n)

        class Emptier:
            def __init__(self, who, first, eng):
                self.who, self.first, self.n, self.eng = who, first, 0, eng

            def take(self):
                self.eng.wait_ge(S(f"{self.who}_filled"), self.n + 1)
                self.n += 1
                return bank[self.first + (self.n - 1) % 4]

            def free(self, ins):
                ins.then_inc(S(f"{self.who}_emptied"), 1)
                self.eng.wait_ge(S(f"{self.who}_emptied"), self.n)

        SWEEPS = [(0, 0), (0, 1), (1, 1)]

        def first_tile(L):
            return 0 if L < DEPTH - 1 else NT // 2

        ORDER = ((0, 1, 2, 3), (1, 0, 3, 2))

        def use(load, slot):
            return 16 * (load // 2 + 1)

        block = ctx.enter_context(nc.Block())

        @block.sync
        def _(sp):
            n = [0]

            def chunk(src):
                k = n[0]
                if k >= 2:
                    sp.wait_ge(S("chunk_used"), k - 1)
                sp.dma_start(stream[:, k % 2, :], src).then_inc(S(f"chunk_in{k % 2}"), 16)
                n[0] += 1

            for c in range(2):
                chunk(A["wada"][c])
            with sp.Fori(1, DEPTH * NADA // 2) as i:
                for c in range(2):
                    sp.wait_ge(S("chunk_used"), 2 * i + c - 1)
                    sp.dma_start(stream[:, c, :], A["wada"][2 * i + c]).then_inc(S(f"chunk_in{c}"), 16)
            n[0] = DEPTH * NADA
            sweep = 0
            for L in range(DEPTH):
                for c in range(NWIN):
                    chunk(A["win"][L * NWIN + c])
                for c in range(NWOUT):
                    chunk(A["wout"][L * NWOUT + c])
                for _ in range(len([x for x in SWEEPS if x[0] == L])):
                    for c in range(NWQ):
                        chunk(A["wq"][L * NWQ + c])
                    base = sweep * 2 * PAIRS

                    def pair(p, s, first):
                        if first:
                            sp.wait_ge(S("chunk_used"), n[0] - 1 + s)
                        else:
                            sp.wait_ge(S("hidden_filled"), base + 2 * p - 2)
                        sp.dma_start(stream[:, s, 0:2048], A["u"][L * PAIRS + p]).then_inc(S(f"u_in{s}"), 16)
                        if not first:
                            sp.wait_ge(S("experts_summed"), base + 2 * p - 2)
                        sp.dma_start(stream[:, s, 2048:4096], A["v"][L * PAIRS + p]).then_inc(S(f"v_in{s}"), 16)

                    pair(0, 0, True)
                    pair(1, 1, True)
                    with sp.Fori(1, PAIRS // 2) as i:
                        pair(2 * i, 0, False)
                        pair(2 * i + 1, 1, False)
                    sp.wait_ge(S("experts_summed"), base + 2 * PAIRS)
                    sweep += 1
            sp.wait_ge(S("normed"), 5)
            for t in range(NT // 2, NT):
                sp.dma_start(out[0, (t - 2) * P:(t - 1) * P, :], X[:, t, :]).then_inc(S("out_stored"), 16)
            sp.wait_ge(S("out_stored"), 32)

        @block.gpsimd
        def _(pool):
            c = Count(pool, "pool_step")
            pool.dma_start(iota[:, :], A["iota"]).then_inc(S("base_in"), 16)
            pool.dma_start(ident[:, :], A["ident"]).then_inc(S("base_in"), 16)
            for t in range(NT):
                src = A["ctx"][0] if t < 2 else A["x"][0]
                pool.dma_start(X[:, t, :], src[(t % 2) * P:(t % 2 + 1) * P, :]).then_inc(S("base_in"), 16)
            pool.dma_start(small[:, 0:8], A["c_cols"]).then_inc(S("cond_in"), 16)
            pool.dma_start(small[:, 8:16], A["cctx_cols"]).then_inc(S("cond_in"), 16)
            pool.dma_start(arena[0:2, 0:DEPTH * 6 * D], A["b_ada"].rearrange("l n -> (l n)").partition_broadcast(2)).then_inc(S("cond_in"), 16)
            with pool.Fori(0, DEPTH * NADA // 4) as i:
                for u in range(4):
                    pool.wait_ge(S("mod_made"), 4 * i + u + 1)
                    pool.dma_start(modd.rearrange("s l (c n) -> s (l c) n", n=512)[:, 4 * i + u, :],
                                   arena[0:2, 16384 + 512 * u:16384 + 512 * (u + 1)]).then_inc(S(f"mod_stored{u}"), 16)
            for u in range(4):
                pool.wait_ge(S(f"mod_stored{u}"), 16 * DEPTH * NADA // 4)
            for L in range(DEPTH):
                if L:
                    pool.wait_ge(S("normed"), 3)
                for r in range(2):
                    pool.dma_start(arena[48 * r:48 * r + 48, place["xb"]:place["xb"] + P],
                                   modd[r, L].rearrange("(v p) -> v p", p=P)).then_inc(S("modrow_in"), 16)
                pool.dma_start(con, A["const"]).then_inc(S("params_in"), 16)
                pool.dma_start(sw, A["smallw"][L]).then_inc(S("params_in"), 16)
                pool.dma_start(col, A["cols"][L]).then_inc(S("params_in"), 16)
                pool.dma_start(row, A["rows"][L].partition_broadcast(P)).then_inc(S("params_in"), 16)
                pool.dma_start(keysT[:, :, :], A["keys"][L]).then_inc(S("params_in"), 16)
                for r in range(2):
                    pool.dma_start(lnr[:, r, :], A["ln"][L, r].partition_broadcast(P)).then_inc(S("params_in"), 16)
                    pool.dma_start(lnr[:, 2 + r, :], modd[r, L, 2 * D:3 * D].partition_broadcast(P)).then_inc(S("params_in"), 16)
                for s, (LL, g) in enumerate(SWEEPS):
                    if LL != L:
                        continue
                    pool.wait_ge(S("gates_filled"), 64 * (s + 1))
                    pool.dma_start(grow[:, 0, :], modd[g, L, 5 * D:6 * D].partition_broadcast(P)).then_inc(S("rows_in"), 16)
                    pool.dma_start(grow[:, 1, :], A["ln"][L, 2].partition_broadcast(P)).then_inc(S("rows_in"), 16)
                    pool.dma_start(grow[:, 2, :], A["ln"][L, 3].partition_broadcast(P)).then_inc(S("rows_in"), 16)

        @block.tensor
        def _(pe):
            c = Count(pe, "pe_step")
            toA, toV = Filler("act", 0), Filler("dve", 4)
            chunks = [0]

            def mm(o, lhsT, rhs, start=True, stop=True):
                return nc.tensor.matmul(o, lhsT, rhs, start=start, stop=stop, skip_group_check=True)

            def tr(o, i):
                return nc.tensor.transpose(o, i, ident[0:i.shape[0], 0:i.shape[0]])

            def chunk_ready():
                k = chunks[0]
                pe.wait_ge(S(f"chunk_in{k % 2}"), use(k, k % 2))
                return split(stream[:, k % 2, :], k=KD, n=512)

            def chunk_done():
                chunks[0] += 1

            def settle():
                toA.settled(pe)
                toV.settled(pe)

            pe.wait_ge(S("base_in"), 16 * 6)
            pe.wait_ge(S("cond_ready"), 1)
            cs = split(small[:, 16:32], s=2, k=KD)

            def ada(i, u, first):
                pe.wait_ge(S(f"chunk_in{u % 2}"), 32 * i + 16 * (u // 2 + 1))
                if not first:
                    pe.wait_ge(S("mod_made"), 4 * i + u - 3)
                w = split(stream[:, u % 2, :], k=KD, n=512)
                for k in range(KD):
                    m = mm(bank[4 + u][0:2, :], cs[:, :, k], w[:, k, :], k == 0, k == KD - 1)
                m.then_inc(S("chunk_used"), 1)

            for u in range(4):
                ada(0, u, True)
            with pe.Fori(1, DEPTH * NADA // 4) as i:
                for u in range(4):
                    ada(i, u, False)
            pe.wait_ge(S("mod_made"), DEPTH * NADA)
            chunks[0] = DEPTH * NADA

            def mixers(L):
                T0 = first_tile(L)
                c.await_("modrow_in", 32)
                b = toV.open(pe)
                toV.close(tr(b[:, 0:96], arena[0:96, place["xb"]:place["xb"] + P]))
                c.await_("mod_columns")
                if L:
                    pe.wait_ge(S("normed"), 3)
                for k in range(KD):
                    ring = toA if k % 2 == 0 else toV
                    b = ring.open(pe)
                    for t in range(NT):
                        m = tr(b[:, t * P:(t + 1) * P], X[:, t, k * P:(k + 1) * P])
                    ring.close(m)
                settle()
                unit = 0
                for ch in range(NWIN):
                    w = chunk_ready()
                    nb = {0: 4, 1: 2}.get(ch, 0)
                    for bl in range(nb):
                        ring = toA if unit % 2 == 0 else toV
                        unit += 1
                        b = ring.open(pe)
                        for k in range(KD):
                            m = mm(b[:, :], w[:, k, bl * P:(bl + 1) * P], xmT[:, k, :], k == 0, k == KD - 1)
                        ring.close(m)
                    lo = nb * P
                    hi = 512 if ch < NWIN - 1 else NPT - 256 - 3 * 512
                    for t in range(NT if lo < hi else 0):
                        ring = toA if unit % 2 == 0 else toV
                        unit += 1
                        b = ring.open(pe)
                        for k in range(KD):
                            m = mm(b[:, 0:hi - lo], xmT[:, k, t * P:(t + 1) * P], w[:, k, lo:hi], k == 0, k == KD - 1)
                        ring.close(m)
                    ring.flushed(pe)
                    pe.sem_inc(S("chunk_used"), 1)
                    chunk_done()

                pe.wait_ge(S("params_in"), 16 * 9 * (L + 1))
                c.await_("mla_latents")
                for k in range(2):
                    b = toA.open(pe)
                    for t in range(NT):
                        m = tr(b[:, t * P:(t + 1) * P], ptok[:, t, O_CQ + k * P:O_CQ + (k + 1) * P])
                    toA.close(m)
                b = toV.open(pe)
                for t in range(NT):
                    m = tr(b[:, t * P:(t + 1) * P], ptok[:, t, O_CKV:O_CKV + P])
                toV.close(m)
                settle()
                for t in range(NT):
                    b = toA.open(pe)
                    mm(b[:, 0:GW], ckvT[:, t * P:(t + 1) * P], wuk)
                    toA.close(mm(b[:, GW:2 * GW], ckvT[:, t * P:(t + 1) * P], wuv))
                    if t >= T0:
                        b = toV.open(pe)
                        for k in range(2):
                            m = mm(b[:, 0:HEADS * QKD], cqT[:, k, t * P:(t + 1) * P], wuq[:, k, :], k == 0, k == 1)
                        toV.close(m)
                c.await_("mla_rotated")
                for h in range(HEADS):
                    b = toA.open(pe)
                    for t in range(NT):
                        m = tr(b[0:QKD, t * P:(t + 1) * P], ktok[:, t, h, :])
                    toA.close(m)
                    b = toV.open(pe)
                    for t in range(T0, NT):
                        m = tr(b[0:QKD, t * P:(t + 1) * P], qtok[:, t, h, :])
                    toV.close(m)
                settle()
                units = [(t, h) for t in range(T0, NT) for h in range(HEADS)]
                ub = 16 * L

                def keys_of(t):
                    return CTX if t < 2 else TOK

                def scores(i):
                    t, h = units[i]
                    if i >= 2:
                        pe.wait_ge(S("probs_ready"), ub + i - 1)
                    mm(bank[i % 2][:, 0:keys_of(t)], qT[0:QKD, h, t * P:(t + 1) * P], kT[0:QKD, h, 0:keys_of(t)]
                       ).then_inc(S("scores_filled"), 1)

                def turn(i):
                    pe.wait_ge(S("probs_ready"), ub + i + 1)
                    if i >= 2:
                        pe.wait_ge(S("turned_emptied"), ub + i - 1)
                    for j in range(keys_of(units[i][0]) // P):
                        m = tr(bank[2 + i % 2][:, j * P:(j + 1) * P], probs[:, i % 2, j * P:(j + 1) * P])
                    m.then_inc(S("turned_filled"), 1)

                def weigh(i):
                    t, h = units[i]
                    n = i // HEADS
                    nk = keys_of(t) // P
                    pe.wait_ge(S("turned_emptied"), ub + i + 1)
                    if h == 0 and n >= 2:
                        pe.wait_ge(S("tile_attended"), ub // HEADS + n - 1)
                    for j in range(nk):
                        m = mm(bank[4 + n % 2][:, h * VD:(h + 1) * VD], pT[:, i % 2, j * P:(j + 1) * P],
                               vtok[:, j, h * VD:(h + 1) * VD], j == 0, j == nk - 1)
                    m.then_inc(S("weighed"), 1)

                scores(0)
                scores(1)
                for i in range(len(units)):
                    turn(i)
                    if i + 2 < len(units):
                        scores(i + 2)
                    weigh(i)
                pe.wait_ge(S("tile_attended"), ub // HEADS + len(units) // HEADS)

                b = toV.open(pe)
                for t in range(NT):
                    m = tr(b[0:32, t * P:(t + 1) * P], ptok[:, t, O_GL:O_GL + 32])
                toV.close(m)
                for o in (O_GQ, O_GK):
                    b = toA.open(pe)
                    for t in range(NT):
                        m = tr(b[:, t * P:(t + 1) * P], ptok[:, t, o:o + P])
                    toA.close(m)
                settle()
                for d in range(2):
                    b = toA.open(pe)
                    toA.close(mm(b[:, :], wg[:, d, :], lrT[0:32, :]))
                c.await_("gla_scaled")
                for d in range(2):
                    b = toA.open(pe)
                    for t in range(NT):
                        m = tr(b[:, t * P:(t + 1) * P], gE2[:, d * TOK + t * P:d * TOK + (t + 1) * P])
                    toA.close(m)
                settle()
                scan_states("gla", lambda d, t: (gKtok[:, d, t, :], ptok[:, t, O_GV:O_GV + GW]))
                for n, t in enumerate(range(T0, NT)):
                    for d in range(2):
                        c.await_("gla_spread")
                        b = toV.open(pe)
                        toV.close(mm(b[:, :], gE2[:, d * TOK + t * P:d * TOK + (t + 1) * P], gQx[:, d, :, :]))
                    toV.settled(pe)
                    b = toA.open(pe)
                    first = True
                    for d in range(2):
                        if t != ORDER[d][0]:
                            m = mm(b[:, 0:GW], gE1[:, d * TOK + t * P:d * TOK + (t + 1) * P], states[:, d, t, :], first, False)
                            first = False
                    for h in range(HEADS):
                        for d in range(2):
                            m = mm(b[:, h * DV:(h + 1) * DV], mats[:, n % 2, d, h * P:(h + 1) * P],
                                   ptok[:, t, O_GV + h * DV:O_GV + (h + 1) * DV], first, d == 1)
                            first = False
                    toA.close(m)
                settle()

                c.await_("ret_rotated")
                for o in (O_RQ, O_RK):
                    b = toA.open(pe)
                    for t in range(NT):
                        m = tr(b[:, t * P:(t + 1) * P], ptok[:, t, o:o + P])
                    toA.close(m)
                settle()
                c.await_("ret_scaled")
                scan_states("ret", lambda d, t: (ptok[:, t, O_RK:O_RK + P], rV[:, d, t, :]))
                for n, t in enumerate(range(T0, NT)):
                    c.await_("ret_spread")
                    b = toV.open(pe)
                    toV.close(mm(b[:, :], rkT[:, t, :], rQx[:, n % 2, :, :]))
                    toV.settled(pe)
                    b = toA.open(pe)
                    first = True
                    for d in range(2):
                        if t != ORDER[d][0]:
                            m = mm(b[:, 0:GW], rQ[:, d, t, :], states[:, d, t, :], first, False)
                            first = False
                    for h in range(HEADS):
                        m = mm(b[:, h * DV:(h + 1) * DV], mats[:, n % 2, 0, h * P:(h + 1) * P],
                               ptok[:, t, O_RV + h * DV:O_RV + (h + 1) * DV], first, True)
                        first = False
                    toA.close(m)
                settle()

                c.await_("ssd_conv")
                for t in range(NT):
                    b = toA.open(pe)
                    for j in range(4):
                        m = tr(b[:, j * P:(j + 1) * P], cvT[:, j, t * P:(t + 1) * P])
                    toA.close(m)
                c.await_("ssd_rates")
                b = toV.open(pe)
                for t in range(NT):
                    for d, mask in enumerate(("maskF", "maskB")):
                        m = mm(b[:, t * 8 + 4 * d:t * 8 + 4 * d + 4], C(mask), s_la[:, t, 4 * d:4 * d + 4])
                toV.close(m)
                b = toV.open(pe)
                toV.close(mm(b[:, 0:32], C("ones"), sm[:, 32:64]))
                settle()
                c.await_("ssd_values")
                scan_states("ssd", None)
                for n, t in enumerate(range(T0, NT)):
                    for d in range(2):
                        c.await_("ssd_masked")
                        b = toV.open(pe)
                        toV.close(mm(b[:, :], C("ones"), laM[:, d, :, :]))
                    b = toV.open(pe)
                    for g in range(2):
                        m = mm(b[:, g * P:(g + 1) * P], cvT[:, 2 + g, t * P:(t + 1) * P], cvT[:, 4 + g, t * P:(t + 1) * P])
                    toV.close(m)
                    c.await_("ssd_decayed")
                    toV.settled(pe)
                    b = toA.open(pe)
                    first = True
                    for h in range(HEADS):
                        o = b[:, h * DV:(h + 1) * DV]
                        for d in range(2):
                            if t != ORDER[d][0]:
                                mm(o, sQ[:, d, h, :], states[:, d, t, h * DV:(h + 1) * DV], first, False)
                                first = False
                        for d in range(2):
                            m = mm(o, sM[:, d, h * P:(h + 1) * P], sV[:, d, t, h * DV:(h + 1) * DV], first, d == 1)
                            first = False
                    toA.close(m)
                settle()

                c.await_("mixed")
                for k in range(KD):
                    ring = toA if k % 2 == 0 else toV
                    o = (O_CQ, O_GQ, O_Z, O_RQ)[k // 2] + (k % 2) * P
                    b = ring.open(pe)
                    for t in range(T0, NT):
                        m = tr(b[:, t * P:(t + 1) * P], ptok[:, t, o:o + P])
                    ring.close(m)
                settle()
                for ch in range(NWOUT):
                    w = chunk_ready()
                    for t in range(T0, NT):
                        b = toV.open(pe)
                        for k in range(KD):
                            m = mm(b[:, :], xmT[:, k, t * P:(t + 1) * P], w[:, k, :], k == 0, k == KD - 1)
                        toV.close(m)
                    toV.flushed(pe)
                    pe.sem_inc(S("chunk_used"), 1)
                    chunk_done()

            def scan_states(kind, operands):
                for step in range(NT - 1):
                    for d in range(2):
                        t = ORDER[d][step]
                        b = toV.open(pe)
                        if operands:
                            k, v = operands(d, t)
                            m = mm(b[:, 0:GW], k, v)
                        else:
                            for g in range(2):
                                m = mm(b[:, g * P:(g + 1) * P], xBtok[:, t, 256 + g * P:256 + (g + 1) * P],
                                       sVw[:, d, t, g * P:(g + 1) * P])
                        toV.close(m)
                c.await_("states_ready")

            def experts(s, L, g):
                pe.wait_ge(S("normed"), (1, 1, 4)[s])
                for k in range(KD):
                    ring = toA if k % 2 == 0 else toV
                    b = ring.open(pe)
                    for t in range(2):
                        m = tr(b[:, t * P:(t + 1) * P], X[:, 2 * g + t, k * P:(k + 1) * P])
                    ring.close(m)
                settle()

                def query(bl):
                    w = split(stream[:, chunks[0] % 2, :], k=KD, n=512)
                    b = toA.open(pe)
                    for k in range(KD):
                        m = mm(b[:, 0:256], w[:, k, (bl % 4) * P:(bl % 4 + 1) * P], xTk[:, k, :], k == 0, k == KD - 1)
                    toA.close(m)

                def key_scores(bl):
                    toA.settled(pe)
                    b = toV.open(pe)
                    for t in range(2):
                        m = mm(b[:, t * P:(t + 1) * P], actv[:, bl % 2, t * P:(t + 1) * P], keysT[:, bl % 2, :])
                    toV.close(m)

                for ch in range(NWQ):
                    chunk_ready()
                    for i in range(4):
                        query(4 * ch + i)
                        key_scores(4 * ch + i)
                    toV.flushed(pe)
                    pe.sem_inc(S("chunk_used"), 1)
                    chunk_done()
                c.await_("picked")
                for w in range(3):
                    b = toV.open(pe)
                    for t in range(2):
                        m = tr(b[:, t * P:(t + 1) * P], sel[:, w, t, :])
                    toV.close(m)
                settle()
                gbase = 64 * s

                def tokens(i, u):
                    n = gbase + 4 * i + u
                    pe.wait_ge(S("hots_ready"), n + 1)
                    if not isinstance(n, int) or n >= 4:
                        pe.wait_ge(S("gates_emptied"), n - 3)
                    for q in range(4):
                        m = mm(bank[u][:, q * P:(q + 1) * P], hotJ[:, u % 2, q, :], hotI[:, u % 2, q, :])
                    m.then_inc(S("gates_filled"), 1)

                for u in range(4):
                    tokens(0, u)
                with pe.Fori(1, 16) as i:
                    for u in range(4):
                        tokens(i, u)
                pe.wait_ge(S("gates_emptied"), gbase + 64)
                base = 2 * PAIRS * s
                lbase = 16 * (PAIRS // 2) * s
                outb = [toV.open(pe) for _ in range(4)]

                def hidden(p, half, sl, q, load):
                    n = base + 2 * p + half
                    if half == 0:
                        pe.wait_ge(S(f"u_in{sl}"), load)
                    if not isinstance(n, int) or n >= 4:
                        pe.wait_ge(S("gelu_done"), n - 3)
                    for k in range(KD):
                        m = mm(bank[q][:, 0:256], stream[:, sl, half * 1024 + k * P:half * 1024 + (k + 1) * P], xTk[:, k, :],
                               k == 0, k == KD - 1)
                    m.then_inc(S("hidden_filled"), 1)

                def summed(p, half, sl, load, first=False, last=False):
                    n = base + 2 * p + half
                    if half == 0:
                        pe.wait_ge(S(f"v_in{sl}"), load)
                    pe.wait_ge(S("act_ready"), n + 1)
                    for t in range(2):
                        for hf in range(2):
                            m = mm(outb[2 * t + hf][:, :], actv[:, 2 + half, t * P:(t + 1) * P],
                                   stream[:, sl, 2048 + half * 1024 + hf * 512:2048 + half * 1024 + (hf + 1) * 512], first, last)
                    m.then_inc(S("experts_summed"), 1)

                def pair(p, i, sl, first=False, last=False):
                    hidden(p, 1, sl, 2 * sl + 1, None)
                    summed(p, 0, sl, lbase + 16 * i + 16, first, False)
                    if not last:
                        hidden(p + 1, 0, 1 - sl, 2 * (1 - sl), lbase + 16 * i + 16 + 16 * sl)
                    summed(p, 1, sl, None, False, last)

                hidden(0, 0, 0, 0, lbase + 16)
                pair(0, 0, 0, first=True)
                pair(1, 0, 1)
                with pe.Fori(1, PAIRS // 2 - 1) as i:
                    pair(2 * i, i, 0)
                    pair(2 * i + 1, i, 1)
                pair(PAIRS - 2, PAIRS // 2 - 1, 0)
                pair(PAIRS - 1, PAIRS // 2 - 1, 1, last=True)
                pe.wait_ge(S("experts_summed"), base + 2 * PAIRS)
                pe.sem_inc(S("dve_filled"), 4)

            s = 0
            for L in range(DEPTH):
                mixers(L)
                while s < len(SWEEPS) and SWEEPS[s][0] == L:
                    experts(s, *SWEEPS[s])
                    s += 1

        @block.scalar
        def _(act):
            c = Count(act, "act_step")
            ring = Emptier("act", 0, act)
            go = nc.scalar.activation

            act.wait_ge(S("cond_in"), 48)
            c.step(go(small[:, 16:24], small[:, 8:16], ACT.Silu))
            c.step(go(small[:, 24:32], small[:, 0:8], ACT.Silu))
            c.tell("cond_ready")

            def modulated(dst, b, k, s, a, n, v, last):
                ins = go(dst, b[:, a:a + n], ACT.Identity, bias=modc[:, s, v, k:k + 1], scale=modc[:, s, v + 1, k:k + 1])
                if last:
                    ring.free(ins)

            def norm_scale(src, dst, name):
                c.await_(name)
                c.step(go(dst, src, ACT.Ln))
                c.step(go(dst, dst, ACT.Exp, scale=-0.5))
                c.tell(name + "_root")

            def mixers(L):
                T0 = first_tile(L)
                TS = slice(T0, NT)
                c.await_("mod_columns")
                for k in range(0, KD, 2):
                    b = ring.take()
                    modulated(xmT[:, k, 0:CTX], b, k, 0, 0, CTX, 0, False)
                    modulated(xmT[:, k, CTX:TOK], b, k, 1, CTX, SEQ, 0, True)
                units = [("x", b) for b in range(NXB)] + [("t", ch, t) for ch in range(1, NWIN) for t in range(NT)]
                for u in units[::2]:
                    b = ring.take()
                    if u[0] == "x":
                        ring.free(go(xbT[:, u[1], :], b[:, :], ACT.Copy))
                    else:
                        ch, t = u[1:]
                        a = 0 if ch == 1 else 256 + (ch - 2) * 512
                        n = 256 if ch == 1 else min(512, NPT - a)
                        ring.free(go(ptok[:, t, a:a + n], b[:, 0:n], ACT.Copy))
                c.tell("projected_by_act")
                c.await_("projected_by_dve")
                for o in (O_GR, O_Z, O_RG):
                    c.step(go(ptok[:, TS, o:o + GW], ptok[:, TS, o:o + GW], ACT.Silu))
                c.await_("conv_summed")
                c.step(go(cvT[:, :, :], cvT[:, :, :], ACT.Silu))
                c.tell("ssd_conv")
                act.wait_ge(S("params_in"), 16 * 9 * (L + 1))
                for t in range(NT):
                    c.step(go(cqT[:, 0, 0:QLORA], ptok[:, t, O_CQ:O_CQ + QLORA], ACT.Square, accum_out=small[:, 40 + t:41 + t]))
                    c.step(go(cqT[:, 0, 0:KVLORA], ptok[:, t, O_CKV:O_CKV + KVLORA], ACT.Square, accum_out=small[:, 44 + t:45 + t]))
                c.tell("latent_squares")
                norm_scale(small[:, 32:40], small[:, 40:48], "latent_meansq")
                for k in range(2):
                    b = ring.take()
                    ring.free(go(cqT[:, k, :], b[:, :], ACT.Copy, scale=col[:, C_GQ + k:C_GQ + k + 1]))
                for t in range(NT):
                    b = ring.take()
                    go(ktok[:, t, :, 0:NOPE], split(b[:, 0:GW], h=HEADS, n=NOPE), ACT.Copy)
                    ring.free(go(vtok[:, t, :], b[:, GW:2 * GW], ACT.Copy))
                c.tell("mla_keys")
                for h in range(HEADS):
                    b = ring.take()
                    ring.free(go(kT[0:QKD, h, :], b[0:QKD, :], ACT.Copy))
                units = [(t, h) for t in range(T0, NT) for h in range(HEADS)]
                for i, (t, h) in enumerate(units):
                    nk = CTX if t < 2 else TOK
                    act.wait_ge(S("row_max"), 16 * L + i + 1)
                    if i >= 2:
                        act.wait_ge(S("turned_filled"), 16 * L + i - 1)
                    go(probs[:, i % 2, 0:nk], bank[i % 2][:, 0:nk], ACT.Exp, bias=small[:, 64 + i:65 + i],
                       accum_out=small[:, 48 + i:49 + i]).then_inc(S("probs_ready"), 1)

                b = ring.take()
                ring.free(go(gqT, b[:, :], ACT.Copy, scale=DK ** -0.5))
                b = ring.take()
                ring.free(go(gkT, b[:, :], ACT.Copy))
                for d in range(2):
                    b = ring.take()
                    ring.free(go(gz[:, d * TOK:(d + 1) * TOK], b[:, :], ACT.Identity, bias=col[:, C_BGF + d:C_BGF + d + 1]))
                c.step(go(ge, gz, ACT.Abs))
                c.step(go(ge, ge, ACT.Exp, scale=-1.0))
                c.step(go(ge, ge, ACT.Ln, bias=1.0))
                c.tell("gla_logs")
                c.await_("gla_cums")
                c.step(go(gE1, ge, ACT.Exp, scale=1.0 / 16))
                c.step(go(gE2, ge, ACT.Exp, scale=-1.0 / 16))
                c.step(go(small[:, 112:136], small[:, 112:136], ACT.Exp, scale=1.0 / 16))
                c.tell("gla_exps")
                for d in range(2):
                    b = ring.take()
                    ring.free(go(gKtok[:, d, :, :], split(b[:, :], t=NT, n=P), ACT.Copy))
                for t in range(T0, NT):
                    b = ring.take()
                    ring.free(go(ptok[:, t, O_GQ:O_GQ + GW], b[:, 0:GW], ACT.Copy))
                c.tell("gla_outs")
                norm_scale(small[:, 80:96], small[:, 96:112], "gla_meansq")

                b = ring.take()
                ring.free(go(rqT, split(b[:, :], t=NT, n=P), ACT.Copy, scale=DK ** -0.5))
                b = ring.take()
                ring.free(go(rkT, split(b[:, :], t=NT, n=P), ACT.Copy))
                c.tell("ret_turned")
                for t in range(T0, NT):
                    b = ring.take()
                    ring.free(go(ptok[:, t, O_RQ:O_RQ + GW], b[:, 0:GW], ACT.Copy))
                c.tell("ret_outs")
                norm_scale(small[:, 80:96], small[:, 96:112], "ret_meansq")

                for t in range(NT):
                    b = ring.take()
                    ring.free(go(xBtok[:, t, :], b[:, :], ACT.Copy))
                c.await_("ssd_rates_raw")
                c.step(go(s_t, s_dt, ACT.Abs))
                c.step(go(s_t, s_t, ACT.Exp, scale=-1.0))
                c.step(go(s_t, s_t, ACT.Ln, bias=1.0))
                c.step(go(small[:, 136:144], row[:, R_ALOG:R_ALOG + 8], ACT.Exp))
                c.tell("ssd_logs")
                c.await_("ssd_sums")
                c.step(go(s_w, s_w, ACT.Exp))
                c.step(go(s_el, s_t, ACT.Exp))
                c.tell("ssd_decays")
                for t in range(T0, NT):
                    c.await_("ssd_exponents")
                    c.step(go(sE, sE, ACT.Exp))
                    c.step(go(sD, sD, ACT.Exp))
                    c.tell("ssd_exps")
                    b = ring.take()
                    ring.free(go(sVw[:, 0, t, :], b[:, 0:GW], ACT.Copy))
                c.tell("ssd_outs")
                norm_scale(small[:, 80:84], small[:, 96:100], "ssd_meansq")

                for k in range(0, KD, 2):
                    b = ring.take()
                    ring.free(go(xmT[:, k, T0 * P:TOK], b[:, T0 * P:TOK], ACT.Copy))
                norm_scale(small[:, 132:136], small[:, 136:140], "ln_var")

            def experts(s, L, g):
                for k in range(0, KD, 2):
                    b = ring.take()
                    modulated(xTk[:, k, :], b, k, g, 0, 256, 3, True)
                for bl in range(2 * PH):
                    b = ring.take()
                    if bl >= 2:
                        act.wait_ge(S("query_used"), 2 * PH * s + bl - 1)
                    ring.free(go(actv[:, bl % 2, :], b[:, 0:256], ACT.Copy))
                c.await_("softmax_shifted")
                c.step(go(vsel, vsel, ACT.Exp))
                c.tell("softmax_exps")
                gb = 64 * s

                def empty_gates(i, u):
                    n = gb + 4 * i + u
                    act.wait_ge(S("gates_filled"), n + 1)
                    go(gates[:, bass.ds(16 * i + 4 * u, 4), :], split(bank[u][:, :], t=4, i=P), ACT.Copy).then_inc(S("gates_emptied"), 1)

                with act.Fori(0, 16) as i:
                    for u in range(4):
                        empty_gates(i, u)
                base = 2 * PAIRS * s

                def gelu(p, half, q):
                    n = base + 2 * p + half
                    act.wait_ge(S("hidden_filled"), n + 1)
                    if not isinstance(n, int) or n >= 2:
                        act.wait_ge(S("act_ready"), n - 1)
                    go(actv[:, half, :], bank[q][:, 0:256], ACT.Gelu).then_inc(S("gelu_done"), 1)

                for q in range(4):
                    gelu(q // 2, q % 2, q)
                with act.Fori(1, PAIRS // 2) as i:
                    for q in range(4):
                        gelu(2 * i + q // 2, q % 2, q)
                norm_scale(small[:, 132:134], small[:, 136:138], "ln_var")

            s = 0
            for L in range(DEPTH):
                mixers(L)
                while s < len(SWEEPS) and SWEEPS[s][0] == L:
                    experts(s, *SWEEPS[s])
                    s += 1

        @block.vector
        def _(dve):
            c = Count(dve, "dve_step")
            ring = Emptier("dve", 4, dve)
            V = nc.vector

            def tt(o, a, b, op):
                return V.tensor_tensor(o, a, b, op)

            def layer_norm(tiles, b_rows, products, gate_of, g_row):
                for t, hf in products:
                    x = X[:, t, hf * 512:(hf + 1) * 512]
                    b = ring.take()
                    tmp = b_rows
                    ins = tt(tmp, b[:, :], gate_of(t)[:, hf * 512:(hf + 1) * 512], ALU.mult)
                    ring.free(ins)
                    c.step(V.scalar_tensor_tensor(x, x, ALPHA, tmp, ALU.mult, ALU.add))
                for n, t in enumerate(tiles):
                    for hf in range(2):
                        c.step(V.bn_stats(small[:, 112 + 6 * hf:118 + 6 * hf], X[:, t, hf * 512:(hf + 1) * 512]))
                    c.step(V.bn_aggr(small[:, 124 + 2 * n:126 + 2 * n], small[:, 112:124]))
                    c.step(V.tensor_scalar(small[:, 132 + n:133 + n], small[:, 125 + 2 * n:126 + 2 * n], 1e-5, None, ALU.add))
                c.tell("ln_var")
                c.await_("ln_var_root")
                for n, t in enumerate(tiles):
                    c.step(V.tensor_scalar(X[:, t, :], X[:, t, :], small[:, 124 + 2 * n:125 + 2 * n], small[:, 136 + n:137 + n],
                                           ALU.subtract, ALU.mult))
                for r, op in enumerate((ALU.mult, ALU.add)):
                    for t in tiles:
                        c.step(tt(X[:, t, :], X[:, t, :], g_row(r), op))
                c.tell("normed")

            def ada(i, u, first):
                dve.wait_ge(S("chunk_used"), 4 * i + u + 1)
                if not first:
                    dve.wait_ge(S(f"mod_stored{u}"), 16 * i)
                tt(arena[0:2, 16384 + 512 * u:16384 + 512 * (u + 1)], bank[4 + u][0:2, :],
                   arena[0:2, bass.ds(2048 * i + 512 * u, 512)], ALU.add).then_inc(S("mod_made"), 1)

            dve.wait_ge(S("cond_in"), 48)
            for u in range(4):
                ada(0, u, True)
            with dve.Fori(1, DEPTH * NADA // 4) as i:
                for u in range(4):
                    ada(i, u, False)

            def modulated(dst, b, k, s, a, n, v, last):
                ins = V.tensor_scalar(dst, b[:, a:a + n], modc[:, s, v + 1, k:k + 1], modc[:, s, v, k:k + 1], ALU.mult, ALU.add)
                if last:
                    ring.free(ins)

            def head_scale(o, T0, centre, g_row, gate, name):
                n = NT - T0
                x = ptok[:, T0:NT, o:o + GW]
                heads = n * HEADS

                def by_head(ap):
                    return ap.rearrange("p t (h v) -> p t h v", h=HEADS)

                stat = small[:, 80:80 + heads]
                stat4 = split(stat, t=n, h=HEADS)
                shape = [P, n, HEADS, DV]
                sq = norm_sq[:, T0:NT, :]
                if centre:
                    c.step(V.tensor_reduce(stat4, by_head(x), AX.X, ALU.add))
                    c.step(V.tensor_scalar(stat, stat, 1.0 / DV, None, ALU.mult))
                    c.step(tt(by_head(x), by_head(x), spread(stat4, shape, 3), ALU.subtract))
                c.step(tt(sq, x, x, ALU.mult))
                c.step(V.tensor_reduce(stat4, by_head(sq), AX.X, ALU.add))
                c.step(V.tensor_scalar(small[:, 80:96], small[:, 80:96], 1.0 / DV, 1e-6, ALU.mult, ALU.add))
                c.tell(name)
                c.await_(name + "_root")
                c.step(tt(by_head(x), by_head(x), spread(split(small[:, 96:96 + heads], t=n, h=HEADS), shape, 3), ALU.mult))
                if g_row is not None:
                    c.step(tt(x, x, spread(g_row, [P, n, GW], 1), ALU.mult))
                c.step(tt(x, x, ptok[:, T0:NT, gate:gate + GW], ALU.mult))

            def mixers(L):
                T0 = first_tile(L)
                n_out = NT - T0
                b = ring.take()
                ring.free(V.tensor_copy(modc[:, :, :, :], split(b[:, 0:96], s=2, v=6, k=KD)))
                for v in (1, 4):
                    c.step(V.tensor_scalar(modc[:, :, v, :], modc[:, :, v, :], 1.0, None, ALU.add))
                if L == 0:
                    c.step(V.memset(small[:, 80:96], 1.0))
                c.tell("mod_columns")
                for k in range(1, KD, 2):
                    b = ring.take()
                    modulated(xmT[:, k, 0:CTX], b, k, 0, 0, CTX, 0, False)
                    modulated(xmT[:, k, CTX:TOK], b, k, 1, CTX, SEQ, 0, True)
                units = [("x", b) for b in range(NXB)] + [("t", ch, t) for ch in range(1, NWIN) for t in range(NT)]
                for u in units[1::2]:
                    b = ring.take()
                    if u[0] == "x":
                        ring.free(V.tensor_copy(xbT[:, u[1], :], b[:, :]))
                    else:
                        ch, t = u[1:]
                        a = 0 if ch == 1 else 256 + (ch - 2) * 512
                        n = 256 if ch == 1 else min(512, NPT - a)
                        ring.free(V.tensor_copy(ptok[:, t, a:a + n], b[:, 0:n]))
                c.tell("projected_by_dve")
                c.await_("projected_by_act")
                dve.wait_ge(S("params_in"), 16 * 9 * (L + 1))
                for bl in range(NXB):
                    w = [col[:, C_CW + 3 * bl + j:C_CW + 3 * bl + j + 1] for j in range(3)]
                    xs = split(xbT[:, bl, :], s=2, t=CTX)
                    ys = split(cvT[:, bl, :], s=2, t=CTX)
                    c.step(V.tensor_scalar(ys, xs, w[1], col[:, C_CB + bl:C_CB + bl + 1], ALU.mult, ALU.add))
                    c.step(V.scalar_tensor_tensor(ys[:, :, 1:CTX], xs[:, :, 0:CTX - 1], w[0], ys[:, :, 1:CTX], ALU.mult, ALU.add))
                    c.step(V.scalar_tensor_tensor(ys[:, :, 0:CTX - 1], xs[:, :, 1:CTX], w[2], ys[:, :, 0:CTX - 1], ALU.mult, ALU.add))
                c.tell("conv_summed")

                c.await_("latent_squares")
                c.step(V.tensor_scalar(small[:, 32:36], small[:, 40:44], 1.0 / QLORA, 1e-6, ALU.mult, ALU.add))
                c.step(V.tensor_scalar(small[:, 36:40], small[:, 44:48], 1.0 / KVLORA, 1e-6, ALU.mult, ALU.add))
                c.tell("latent_meansq")
                c.await_("latent_meansq_root")
                for t in range(NT):
                    for w, (o, n) in enumerate(((O_CQ, QLORA), (O_CKV, KVLORA))):
                        c.step(V.tensor_scalar(ptok[:, t, o:o + n], ptok[:, t, o:o + n], small[:, 40 + 4 * w + t:41 + 4 * w + t],
                                               None, ALU.mult))
                c.tell("mla_latents")
                kr = ptok[:, :, O_KR:O_KR + ROPE]
                cosA, sinA = split(C("cosA"), t=NT, n=ROPE), split(C("sinA"), t=NT, n=ROPE)
                hr = ROPE // 2
                c.step(tt(ropeA[:, :, 0, :], kr, cosA, ALU.mult))
                c.step(tt(ropeB[:, :, 0, :], kr, sinA, ALU.mult))
                for h in range(HEADS):
                    c.step(tt(ktok[:, :, h, NOPE:NOPE + hr], ropeA[:, :, 0, 0:hr], ropeB[:, :, 0, hr:ROPE], ALU.subtract))
                    c.step(tt(ktok[:, :, h, NOPE + hr:QKD], ropeB[:, :, 0, 0:hr], ropeA[:, :, 0, hr:ROPE], ALU.add))
                b = ring.take()
                ring.free(V.tensor_scalar(ckvT, b[:, :], col[:, C_GKV:C_GKV + 1], None, ALU.mult))
                for t in range(T0, NT):
                    b = ring.take()
                    ring.free(V.tensor_copy(qtok[:, t, :, :], split(b[:, 0:HEADS * QKD], h=HEADS, n=QKD)))
                qr = qtok[:, T0:NT, :, NOPE:QKD]
                rshape = [P, n_out, HEADS, ROPE]
                rA_, rB_ = ropeA[:, T0:NT], ropeB[:, T0:NT]
                c.step(tt(rA_, qr, spread(cosA[:, T0:NT, :], rshape, 2), ALU.mult))
                c.step(tt(rB_, qr, spread(sinA[:, T0:NT, :], rshape, 2), ALU.mult))
                c.step(tt(qr[:, :, :, 0:hr], rA_[:, :, :, 0:hr], rB_[:, :, :, hr:ROPE], ALU.subtract))
                c.step(tt(qr[:, :, :, hr:ROPE], rB_[:, :, :, 0:hr], rA_[:, :, :, hr:ROPE], ALU.add))
                c.await_("mla_keys")
                c.tell("mla_rotated")
                for h in range(HEADS):
                    b = ring.take()
                    ring.free(V.tensor_scalar(qT[0:QKD, h, T0 * P:TOK], b[0:QKD, T0 * P:TOK], QKD ** -0.5, None, ALU.mult))
                units = [(t, h) for t in range(T0, NT) for h in range(HEADS)]
                ub = 16 * L

                def row_max(i):
                    nk = CTX if units[i][0] < 2 else TOK
                    dve.wait_ge(S("scores_filled"), ub + i + 1)
                    V.tensor_reduce(small[:, 64 + i:65 + i], bank[i % 2][:, 0:nk], AX.X, ALU.max, negate=True
                                    ).then_inc(S("row_max"), 1)

                row_max(0)
                row_max(1)
                for i, (t, h) in enumerate(units):
                    nk = CTX if t < 2 else TOK
                    dve.wait_ge(S("turned_filled"), ub + i + 1)
                    if i >= 2:
                        dve.wait_ge(S("weighed"), ub + i - 1)
                    V.tensor_copy(pT[:, i % 2, 0:nk], bank[2 + i % 2][:, 0:nk]).then_inc(S("turned_emptied"), 1)
                    if i + 2 < len(units):
                        row_max(i + 2)
                    if h == HEADS - 1:
                        n = i // HEADS
                        inv = small[:, 104:108]
                        dve.wait_ge(S("probs_ready"), ub + i + 1)
                        c.step(V.reciprocal(inv, small[:, 48 + i - 3:49 + i]))
                        dve.wait_ge(S("weighed"), ub + i + 1)
                        tt(split(ptok[:, t, O_CQ:O_CQ + GW], h=HEADS, n=VD), split(bank[4 + n % 2][:, 0:GW], h=HEADS, n=VD),
                           spread(inv, [P, HEADS, VD], 2), ALU.mult).then_inc(S("tile_attended"), 1)
                        dve.wait_ge(S("tile_attended"), ub // HEADS + n + 1)

                b = ring.take()
                ring.free(V.tensor_copy(lrT[0:32, :], b[0:32, :]))
                c.await_("gla_logs")
                c.step(V.scalar_tensor_tensor(gz, gz, 0.0, ge, ALU.min, ALU.subtract))
                gcv = split(gc, d=2, t=NT, i=P)
                gzv = split(gz, d=2, t=NT, i=P)
                for t in range(NT):
                    c.step(V.tensor_tensor_scan(gcv[:, 0, t, :], C("ones"), gzv[:, 0, t, :], 0.0, ALU.mult, ALU.add))
                    c.step(V.tensor_tensor_scan(gcv[:, 1, t, ::-1], C("ones"), gzv[:, 1, t, ::-1], 0.0, ALU.mult, ALU.add))
                gs = split(small[:, 112:136], w=3, d=2, t=NT)
                for d in range(2):
                    c.step(V.tensor_copy(gs[:, 0, d, :], gcv[:, d, :, P // 2 - 1 + d]))
                    c.step(V.tensor_copy(gs[:, 1, d, :], gcv[:, d, :, P - 1 if d == 0 else 0]))
                c.step(tt(gs[:, 2], gs[:, 1], gs[:, 0], ALU.subtract))
                c.step(tt(split(ge, w=8, i=P), split(gc, w=8, i=P), spread(small[:, 112:120], [P, 8, P], 2), ALU.subtract))
                c.tell("gla_cums")
                c.await_("gla_exps")
                c.step(tt(split(gE1, d=2, t=TOK), split(gE1, d=2, t=TOK), spread(gqT, [P, 2, TOK], 1), ALU.mult))
                c.step(tt(split(gE2, d=2, t=TOK), split(gE2, d=2, t=TOK), spread(gkT, [P, 2, TOK], 1), ALU.mult))
                c.tell("gla_scaled")
                for st in range(NT - 1):
                    for d in range(2):
                        t, nxt = ORDER[d][st], ORDER[d][st + 1]
                        b = ring.take()
                        s_now, tmp = work[:, d, :], work[:, 2 + d, :]
                        ring.free(V.scalar_tensor_tensor(s_now if st == 0 else tmp, b[:, 0:GW], gs[:, 2, d, t:t + 1], C("blockdiag"),
                                                         ALU.mult, ALU.mult))
                        if st:
                            c.step(V.scalar_tensor_tensor(s_now, s_now, gs[:, 1, d, t:t + 1], tmp, ALU.mult, ALU.add))
                        c.step(V.tensor_scalar(states[:, d, nxt, :], s_now, gs[:, 0, d, nxt:nxt + 1], None, ALU.mult))
                c.tell("states_ready")
                hshape = [P, HEADS, P]
                for n, t in enumerate(range(T0, NT)):
                    for d in range(2):
                        c.step(tt(gQx[:, d, :, :], spread(gE1[:, d * TOK + t * P:d * TOK + (t + 1) * P], hshape, 1),
                                  spread(C("headmask"), hshape, 2), ALU.mult))
                        c.tell("gla_spread")
                    for d, mask in enumerate(("maskF", "maskB")):
                        b = ring.take()
                        ring.free(tt(split(mats[:, n % 2, d, :], h=HEADS, i=P), split(b[:, :], h=HEADS, i=P),
                                     spread(C(mask), hshape, 1), ALU.mult))
                c.await_("gla_outs")
                head_scale(O_GQ, T0, False, row[:, R_GLA:R_GLA + GW], O_GR, "gla_meansq")

                qk = ptok[:, :, O_RQ:O_RQ + 256].rearrange("p t (h n) -> p t h n", n=DK)
                for o, tab in ((rA, "cosR"), (rB, "sinR")):
                    c.step(tt(o, qk, spread(split(C(tab), t=NT, n=DK), [P, NT, 8, DK], 2), ALU.mult))
                c.step(tt(qk[:, :, :, 0:16], rA[:, :, :, 0:16], rB[:, :, :, 16:32], ALU.subtract))
                c.step(tt(qk[:, :, :, 16:32], rB[:, :, :, 0:16], rA[:, :, :, 16:32], ALU.add))
                c.tell("ret_rotated")
                for d, w in enumerate(("retWF", "retWB")):
                    for t in range(NT):
                        c.step(tt(split(rV[:, d, t, :], h=HEADS, v=DV), split(ptok[:, t, O_RV:O_RV + GW], h=HEADS, v=DV),
                                  spread(C(w), [P, HEADS, DV], 2), ALU.mult))
                c.await_("ret_turned")
                for d, w in enumerate(("retQF", "retQB")):
                    c.step(tt(rQ[:, d], rqT, spread(C(w), [P, NT, P], 1), ALU.mult))
                c.tell("ret_scaled")
                for st in range(NT - 1):
                    for d in range(2):
                        t, nxt = ORDER[d][st], ORDER[d][st + 1]
                        b = ring.take()
                        o = states[:, d, nxt, :] if st == 0 else work[:, d, :]
                        ring.free(tt(o, b[:, 0:GW], C("blockdiag"), ALU.mult))
                        if st:
                            c.step(V.scalar_tensor_tensor(states[:, d, nxt, :], states[:, d, t, :], C("retDec"), o, ALU.mult, ALU.add))
                c.tell("states_ready")
                for n, t in enumerate(range(T0, NT)):
                    c.step(tt(rQx[:, n % 2], spread(rqT[:, t, :], hshape, 1), spread(C("headmask"), hshape, 2), ALU.mult))
                    c.tell("ret_spread")
                    b = ring.take()
                    ring.free(tt(mats[:, n % 2, 0, :], b[:, :], C("retD"), ALU.mult))
                c.await_("ret_outs")
                head_scale(O_RQ, T0, True, None, O_RG, "ret_meansq")

                tshape = [P, NT, 8]
                c.step(tt(s_dt, ptok[:, :, O_DT:O_DT + 8], spread(row[:, R_DTB:R_DTB + 8], tshape, 1), ALU.add))
                c.tell("ssd_rates_raw")
                c.await_("ssd_logs")
                c.step(V.scalar_tensor_tensor(s_dt, s_dt, 0.0, s_t, ALU.max, ALU.add))
                c.step(V.scalar_tensor_tensor(s_la, s_dt, -1.0, spread(small[:, 136:144], tshape, 1), ALU.mult, ALU.mult))
                c.tell("ssd_rates")
                b = ring.take()
                ring.free(V.tensor_copy(s_cum, split(b[:, 0:32], t=NT, n=8)))
                b = ring.take()
                ring.free(V.tensor_copy(s_t, split(b[:, 0:32], t=NT, n=8)))
                c.step(tt(s_w, s_t, s_cum, ALU.subtract))
                c.tell("ssd_sums")
                c.await_("ssd_decays")
                c.step(tt(s_w, s_w, s_dt, ALU.mult))
                vshape = [P, NT, HEADS, DV]
                xh = xBtok[:, :, 0:GW].rearrange("p t (h v) -> p t h v", h=HEADS)
                for d in range(2):
                    for o, w in ((sV, s_dt), (sVw, s_w)):
                        c.step(tt(o[:, d].rearrange("p t (h v) -> p t h v", h=HEADS), xh,
                                  spread(w[:, :, 4 * d:4 * d + 4], vshape, 3), ALU.mult))
                c.tell("ssd_values")
                for st in range(NT - 1):
                    for d in range(2):
                        t, nxt = ORDER[d][st], ORDER[d][st + 1]
                        b = ring.take()
                        if st == 0:
                            ring.free(V.tensor_copy(states[:, d, nxt, :], b[:, 0:GW]))
                        else:
                            c.step(tt(split(states[:, d, nxt, :], h=HEADS, v=DV), split(states[:, d, t, :], h=HEADS, v=DV),
                                      spread(s_el[:, t, 4 * d:4 * d + 4], [P, HEADS, DV], 2), ALU.mult))
                            ring.free(tt(states[:, d, nxt, :], states[:, d, nxt, :], b[:, 0:GW], ALU.add))
                c.tell("states_ready")
                for t in range(T0, NT):
                    for d, mask in enumerate(("maskF", "maskB")):
                        c.step(tt(laM[:, d], spread(C(mask), hshape, 1), spread(s_la[:, t, 4 * d:4 * d + 4], hshape, 2), ALU.mult))
                        c.tell("ssd_masked")
                    for d, neg in enumerate(("negF", "negB")):
                        b = ring.take()
                        ring.free(V.tensor_copy(sE[:, d], split(b[:, :], h=HEADS, i=P)))
                        c.step(tt(sD[:, d], sE[:, d], spread(s_cum[:, t, 4 * d:4 * d + 4], hshape, 2), ALU.subtract))
                        c.step(tt(sD[:, d], sD[:, d], spread(C(neg), hshape, 1), ALU.add))
                    c.tell("ssd_exponents")
                    c.await_("ssd_exps")
                    gshape = [P, 2, 2, P]
                    b = ring.take()
                    for d in range(2):
                        c.step(tt(sQ[:, d].rearrange("p (g e) i -> p g e i", g=2), spread(cvT[:, 4:6, t * P:(t + 1) * P], gshape, 2),
                                  sE[:, d].rearrange("p (g e) i -> p g e i", g=2), ALU.mult))
                    for d in range(2):
                        ins = tt(split(sM[:, d, :], g=2, e=2, i=P), spread(split(b[:, 0:256], g=2, i=P), gshape, 2),
                                 sD[:, d].rearrange("p (g e) i -> p g e i", g=2), ALU.mult)
                        if d == 0:
                            c.step(ins)
                        else:
                            ring.free(ins)
                    c.tell("ssd_decayed")
                c.await_("ssd_outs")
                xh = xBtok[:, T0:NT, 0:GW].rearrange("p t (h v) -> p t h v", h=HEADS)
                vshape = [P, n_out, HEADS, DV]
                dsk = row[:, R_DSK:R_DSK + HEADS].unsqueeze(1).unsqueeze(3).to_broadcast(vshape)
                y = xBtok[:, T0:NT, 0:GW]
                zc = ptok[:, T0:NT, O_Z:O_Z + GW]
                c.step(tt(xh, xh, dsk, ALU.mult))
                c.step(tt(y, y, sVw[:, 0, T0:NT, :], ALU.add))
                c.step(tt(zc, zc, y, ALU.mult))
                c.step(tt(norm_sq[:, T0:NT, :], zc, zc, ALU.mult))
                if T0:
                    c.step(V.memset(small[:, 80:84], 1.0))
                c.step(V.tensor_reduce(small[:, 80:80 + n_out], norm_sq[:, T0:NT, :], AX.X, ALU.add))
                c.step(V.tensor_scalar(small[:, 80:84], small[:, 80:84], 1.0 / GW, 1e-6, ALU.mult, ALU.add))
                c.tell("ssd_meansq")
                c.await_("ssd_meansq_root")
                c.step(tt(zc, zc, spread(small[:, 96:96 + n_out], [P, n_out, GW], 2), ALU.mult))
                c.step(tt(zc, zc, spread(row[:, R_SSD:R_SSD + GW], [P, n_out, GW], 1), ALU.mult))
                c.tell("mixed")
                for k in range(1, KD, 2):
                    b = ring.take()
                    ring.free(V.tensor_copy(xmT[:, k, T0 * P:TOK], b[:, T0 * P:TOK]))
                tiles = list(range(T0, NT))
                if T0:
                    c.step(V.memset(small[:, 132:136], 1.0))
                layer_norm(tiles, scratch(W2, 512), [(t, hf) for hf in range(2) for t in tiles],
                           lambda t: lnr[:, 2 + t // 2, :], lambda r: lnr[:, r, :])

            def experts(s, L, g):
                for k in range(1, KD, 2):
                    b = ring.take()
                    modulated(xTk[:, k, :], b, k, g, 0, 256, 3, True)
                def top16(vals_, idx_, src, spare, release):
                    c.step(V.max(vals_[:, 0:8], src))
                    c.step(V.max_index(idx_[:, 0:8], vals_[:, 0:8], src))
                    ins = V.match_replace(spare, vals_[:, 0:8], src, -3.0e38)
                    if release:
                        ring.free(ins)
                    else:
                        c.step(ins)
                    c.step(V.max(vals_[:, 8:16], spare))
                    c.step(V.max_index(idx_[:, 8:16], vals_[:, 8:16], spare))

                for bl in range(2 * PH):
                    b = ring.take()
                    for t in range(2):
                        top16(vals[:, t, bl, :], idxu[:, t, bl, :], b[:, t * P:(t + 1) * P], ctmp[:, 0:P], t == 1)
                    dve.sem_inc(S("query_used"), 1)
                c.step(V.tensor_copy(idxf, idxu))
                cshape = [P, PH, 16, 16]
                for t in range(2):
                    v4 = vals[:, t].rearrange("p (h w) n -> p h w n", w=2)
                    c.step(tt(cand.rearrange("p h (a b) -> p h a b", a=16), spread(v4[:, :, 0, :], cshape, 3),
                              spread(v4[:, :, 1, :], cshape, 2), ALU.add))
                    for h in range(PH):
                        top16(vsel[:, t, h, :], cidxu[:, t, h, :], cand[:, h, :], ctmp, False)
                sshape = [P, 2, PH, 16]
                c.step(V.tensor_copy(small[:, 112:128], vsel[:, :, :, 0].rearrange("p t h -> p (t h)"))
                       if False else V.tensor_copy(split(small[:, 112:128], t=2, h=PH), vsel[:, :, :, 0]))
                c.step(tt(vsel, vsel, spread(split(small[:, 112:128], t=2, h=PH), sshape, 3), ALU.subtract))
                c.tell("softmax_shifted")
                c.step(V.tensor_scalar(cab[:, 0:256], cidx, 4, None, ALU.logical_shift_right))
                c.step(V.tensor_scalar(cab[:, 256:512], cidx, 15, None, ALU.bitwise_and))
                c.step(V.tensor_copy(cabf, cab))
                cab5 = split(cabf, w=2, t=2, h=PH, k=16)
                i16 = iota[:, 0:16].unsqueeze(1).unsqueeze(1).to_broadcast([P, PH, 16, 16])
                for t in range(2):
                    i4 = idxf[:, t].rearrange("p (h w) n -> p h w n", w=2)
                    for w in range(2):
                        c.step(tt(eq, spread(cab5[:, w, t], cshape, 3), i16, ALU.is_equal))
                        c.step(tt(eq, eq, spread(i4[:, :, w, :], cshape, 2), ALU.mult))
                        c.step(V.tensor_reduce(split(sel[:, w, t, :], h=PH, k=16), eq, AX.X, ALU.add))
                c.await_("softmax_exps")
                c.step(V.tensor_reduce(split(small[:, 112:128], t=2, h=PH), vsel, AX.X, ALU.add))
                c.step(V.reciprocal(small[:, 128:144], small[:, 112:128]))
                c.step(tt(sel[:, 2].rearrange("p t (h k) -> p t h k", h=PH), vsel,
                          spread(split(small[:, 128:144], t=2, h=PH), sshape, 3), ALU.mult))
                c.tell("picked")
                for w in range(3):
                    b = ring.take()
                    ring.free(V.tensor_copy(picks[:, w, :], b[:, 0:256]))
                gb = 64 * s

                def hots(i, u):
                    n = gb + 4 * i + u
                    if not isinstance(n, int) or n >= 2:
                        dve.wait_ge(S("gates_filled"), n - 1)
                    for q in range(4):
                        at = (16 * i + 4 * u + q)
                        V.tensor_scalar(hotJ[:, u % 2, q, :], iota[:, :], picks[:, 1, bass.ds(at, 1)], None, ALU.is_equal)
                        ins = V.tensor_scalar(hotI[:, u % 2, q, :], iota[:, :], picks[:, 0, bass.ds(at, 1)],
                                              picks[:, 2, bass.ds(at, 1)], ALU.is_equal, ALU.mult)
                    ins.then_inc(S("hots_ready"), 1)

                for u in range(4):
                    hots(0, u)
                with dve.Fori(1, 16) as i:
                    for u in range(4):
                        hots(i, u)
                dve.wait_ge(S("gates_emptied"), gb + 64)
                base = 2 * PAIRS * s

                def weigh(p, half):
                    n = base + 2 * p + half
                    dve.wait_ge(S("gelu_done"), n + 1)
                    if not isinstance(n, int) or n >= 2:
                        dve.wait_ge(S("experts_summed"), n - 1)
                    tt(actv[:, 2 + half, :], actv[:, half, :], gates[:, :, bass.ds(2 * p + half, 1)].rearrange("p t o -> p (t o)"),
                       ALU.mult).then_inc(S("act_ready"), 1)

                for half in range(2):
                    weigh(0, half)
                with dve.Fori(1, PAIRS) as p:
                    for half in range(2):
                        weigh(p, half)
                dve.wait_ge(S("rows_in"), 16 * 3 * (s + 1))
                c.step(V.memset(small[:, 132:136], 1.0))
                layer_norm([2 * g, 2 * g + 1], scratch(0, 512), [(2 * g + t, hf) for t in range(2) for hf in range(2)],
                           lambda t: grow[:, 0, :], lambda r: grow[:, 1 + r, :])

            s = 0
            for L in range(DEPTH):
                mixers(L)
                while s < len(SWEEPS) and SWEEPS[s][0] == L:
                    experts(s, *SWEEPS[s])
                    s += 1


def shape_constants():
    f = np.float32
    out = np.zeros((P, NCONST), f)

    def put(name, a):
        at, n = CONST[name]
        out[:, at:at + n] = np.asarray(a, f).reshape(P, n)

    j, i = np.arange(P)[:, None], np.arange(P)[None, :]
    put("maskF", j <= i)
    put("maskB", j >= i)
    put("negF", np.where(j <= i, 0.0, -1e30))
    put("negB", np.where(j >= i, 0.0, -1e30))
    log_decay = np.log1p(-np.exp2(-5.0 - np.arange(HEADS)))
    power = np.exp(np.abs(i - j)[:, None, :] * log_decay[None, :, None])
    put("retD", power * (1 + (i == j))[:, None, :])
    by_row = np.repeat(log_decay, DK)[:, None]
    put("retQF", np.exp(by_row * (i + 1)))
    put("retQB", np.exp(by_row * (P - i)))
    put("retWF", np.exp(log_decay[None] * (P - 1 - j)))
    put("retWB", np.exp(log_decay[None] * j))
    put("retDec", np.exp(by_row * P))
    head_of_row, head_of_col = np.arange(P)[:, None] // DK, np.arange(GW)[None] // DV
    put("blockdiag", head_of_row == head_of_col)
    put("headmask", head_of_row == np.arange(HEADS)[None])
    put("ones", np.ones((P, P)))

    def table(pos, half):
        freq = (10000.0 ** (-np.arange(half, dtype=f) / f(half))).astype(f)
        ang = pos.astype(f)[:, None] * freq
        return np.cos(ang.astype(np.float64)), np.sin(ang.astype(np.float64))

    n = np.arange(SEQ)
    crow, srow = table(n // GRID_W, ROPE // 4)
    ccol, scol = table(n % GRID_W, ROPE // 4)
    cr, sr = table(n, DK // 2)
    for name, c, rest in (("cosA", np.concatenate([crow, ccol] * 2, 1), 1.0), ("sinA", np.concatenate([srow, scol] * 2, 1), 0.0),
                          ("cosR", np.concatenate([cr] * 2, 1), 1.0), ("sinR", np.concatenate([sr] * 2, 1), 0.0)):
        full = np.concatenate([np.full((CTX, c.shape[1]), rest), c], 0)
        put(name, full.reshape(NT, P, -1).transpose(1, 0, 2))
    return out


def lay_out(a):
    def chunks(w, n):
        L = w.shape[0]
        return np.ascontiguousarray(w.reshape(L, KD, P, n, 512).transpose(0, 3, 2, 1, 4)).reshape(L * n, P, CHUNK)

    L = DEPTH
    rope = np.concatenate([np.arange(0, 8), np.arange(16, 24), np.arange(8, 16), np.arange(24, 32)])
    order = np.concatenate([np.arange(1472, 2240), np.arange(0, 384), 384 + rope, np.arange(416, 1472),
                            np.arange(2240, 3016)])
    win = np.concatenate([a["w_in"][:, :, order], np.zeros((L, D, NWIN * 512 - order.size), np.float32)], 2)
    uq_order = np.concatenate([np.concatenate([np.arange(NOPE), NOPE + rope]) + QKD * h for h in range(HEADS)])
    uq = a["mla_w_uq"][:, :, uq_order].reshape(L, 2, P, HEADS * QKD).transpose(0, 2, 1, 3).reshape(L, P, -1)
    gate_w = np.zeros((L, P, 2, P), np.float32)
    gate_w[:, 0:RANK, 0] = a["gla_w_gf"]
    gate_w[:, RANK:2 * RANK, 1] = a["gla_w_gb"]
    smallw = np.concatenate([uq, a["mla_w_uk"], a["mla_w_uv"], gate_w.reshape(L, P, 2 * P)], 2)
    col = np.zeros((L, P, NCOL), np.float32)
    col[:, :, C_GQ:C_GQ + 2] = a["mla_g_q"].reshape(L, 2, P).transpose(0, 2, 1)
    col[:, :, C_GKV] = a["mla_g_kv"]
    col[:, :, C_BGF], col[:, :, C_BGB] = a["gla_b_gf"], a["gla_b_gb"]
    col[:, :, C_CW:C_CB] = a["ssd_conv_w"].reshape(L, 3, NXB, P).transpose(0, 3, 2, 1).reshape(L, P, 3 * NXB)
    col[:, :, C_CB:] = a["ssd_conv_b"].reshape(L, NXB, P).transpose(0, 2, 1)
    rows = np.concatenate([a[k] for k in ("gla_g", "ssd_g", "ssd_dt_bias_f", "ssd_dt_bias_b", "ssd_a_log_f", "ssd_a_log_b", "ssd_d")], 1)
    u = a["peer_u"].reshape(L * PAIRS, 2, P, KD, P).transpose(0, 4, 1, 3, 2)
    v = a["peer_v"].reshape(L * PAIRS, 2, P, D).transpose(0, 2, 1, 3)
    return {
        "x": a["x"], "ctx": a["ctx"],
        "c_cols": a["c"].reshape(KD, P).T, "cctx_cols": a["c_ctx"].reshape(KD, P).T,
        "wada": chunks(a["w_ada"], NADA), "b_ada": a["b_ada"], "win": chunks(win, NWIN), "wout": chunks(a["w_out"], NWOUT),
        "wq": chunks(a["peer_w_q"], NWQ), "u": u.reshape(L * PAIRS, P, 2048), "v": v.reshape(L * PAIRS, P, 2048),
        "smallw": smallw, "cols": col, "rows": rows, "keys": a["peer_keys"].transpose(0, 3, 1, 2),
        "ln": np.stack([a[k] for k in ("ln1_g", "ln1_b", "ln2_g", "ln2_b")], 1),
        "const": shape_constants(), "ident": np.eye(P, dtype=np.float32),
        "iota": np.tile(np.arange(P, dtype=np.float32), (P, 1)),
    }


def kernel(**inputs):
    import concourse.bacc as _bacc
    from concourse.bass_utils import run_bass_kernel_spmd as _run

    nc = _bacc.Bacc("TRN2", target_bir_lowering=False, num_devices=1)
    arrays, args = {}, {}
    for name, value in lay_out({k: np.asarray(v) for k, v in inputs.items()}).items():
        value = np.ascontiguousarray(value)
        arrays[f"in_{name}_dram"] = value
        args[name] = nc.dram_tensor(f"in_{name}_dram", value.shape, mybir.dt.from_np(value.dtype), kind="ExternalInput").ap()
    out = nc.dram_tensor("out_0_dram", (1, SEQ, D), F32, kind="ExternalOutput").ap()
    build(nc, args, out)
    r = _run(nc, [arrays], core_ids=[0])
    return r.results[0]["out_0_dram"]
```

```python
from contextlib import ExitStack

import concourse.bass as bass
import numpy as np
from concourse import mybir

F32 = mybir.dt.float32
U32 = mybir.dt.uint32
F32R = mybir.dt.float32r
ALU = mybir.AluOpType
ACT = mybir.ActivationFunctionType
AX = mybir.AxisListType

P = 128
D = 1024
KD = D // P
DEPTH = 2
CTX = 256
SEQ = 256
TOK = CTX + SEQ
NT = TOK // P
GRID_W = 64
HEADS = 4
QLORA, KVLORA, NOPE, ROPE, VD = 256, 128, 64, 32, 64
QKD = NOPE + ROPE
DK, DV = 32, 64
RANK = 16
STATE = 128
GW = HEADS * DV
XBC = 768
NXB = XBC // P
ALPHA = (2 * DEPTH) ** 0.25
PH, NKEY, TOPK = 8, 128, 16
HALF = 128
CHUNK = 4096
SBUF_BASE = 16512

O_CQ, O_CKV, O_KR = 0, 256, 384
O_GQ, O_GK, O_GV, O_GR, O_GL = 416, 544, 672, 928, 1184
O_Z, O_DT = 1216, 1472
O_RQ, O_RK, O_RV, O_RG = 1480, 1608, 1736, 1992
NPT = 2248
NWIN = 6
NWOUT = 2
NWQ = 4
NADA = 12
BLOCKS = 128

CONST = {}
_at = 0
for _name, _n in (("maskF", P), ("maskB", P), ("negF", P), ("negB", P), ("retD", HEADS * P), ("retQF", P), ("retQB", P),
                  ("blockdiag", GW), ("headmask", HEADS), ("retWF", HEADS), ("retWB", HEADS), ("retDec", 1),
                  ("ones", P), ("cosA", NT * ROPE), ("sinA", NT * ROPE), ("cosR", NT * DK), ("sinR", NT * DK)):
    CONST[_name] = (_at, _n)
    _at += _n
NCONST = _at
NSW = 2 * HEADS * QKD + 2 * GW + 2 * P
C_GQ, C_GKV, C_BGF, C_BGB, C_CW, C_CB = 0, 2, 3, 4, 5, 5 + 3 * NXB
NCOL = C_CB + NXB
R_GLA, R_SSD, R_DTB, R_ALOG, R_DSK = 0, GW, 2 * GW, 2 * GW + 8, 2 * GW + 16
NROW = R_DSK + 4


def build(nc, A, out):
    ctx = ExitStack()
    with ctx:
        sems = {}

        def S(name):
            if name not in sems:
                sems[name] = ctx.enter_context(nc.semaphore(name))
            return sems[name]

        top = [SBUF_BASE]

        def at(name, shape, dt=F32, over=None):
            where = top[0] if over is None else over
            if over is None:
                top[0] += 4 * int(np.prod(shape[1:]))
            return nc.alloc_sbuf_tensor_at(name, shape, dt, offset=where), where

        arena, _ = at("arena", [P, 32768])
        stream, stream_at = at("stream", [P, 2, CHUNK])
        X, x_at = at("X", [P, NT, D])
        raw, _ = at("raw", [P, 2, 2, D], over=x_at)
        aux, aux_at = at("aux", [P, 5120])
        acts, _ = at("acts", [P, 2, 256])
        actr, _ = at("actr", [P, 2, 2, 256], F32R)
        ident, _ = at("ident", [P, P])
        iota, _ = at("iota", [P, P])
        modc, _ = at("modc", [P, 2, 6, KD])
        keysT, _ = at("keysT", [P, 2, NKEY])
        small, _ = at("small", [P, 160])
        splits, _ = at("splits", [P, 4, 2, D], F32R, over=stream_at)
        xTr, _ = at("xTr", [P, 2, KD, 256], F32R, over=aux_at)
        rows3, xT, picks = aux[:, 0:3072], aux[:, 3072:5120], aux[:, 4096:4864].rearrange("p (w t) -> p w t", w=3)
        flat = stream[:, :, :].rearrange("p s n -> p (s n)")
        bank = [ctx.enter_context(nc.psum_tensor(f"bank{i}", [P, 512], F32)) for i in range(8)]
        xd = nc.dram_tensor("xd", (NT, P, D), F32, kind="Internal").ap()
        modd = nc.dram_tensor("modd", (2, DEPTH, 6 * D), F32, kind="Internal").ap()

        def region(base, n, tensor=arena):
            return tensor[:, base:base + n]

        a0 = 0
        place = {}
        for name, n in (("xm", KD * TOK), ("pt", NT * NPT), ("xb", NXB * TOK), ("cv", NXB * TOK), ("con", NCONST),
                        ("sw", NSW), ("col", NCOL), ("row", NROW), ("ln", 4 * D)):
            place[name] = a0
            a0 += n
        W2 = a0
        assert 32768 - W2 >= 4608, W2
        XM = place["xm"]
        xmT = region(XM, KD * TOK).rearrange("p (k t) -> p k t", k=KD)
        ptok = region(place["pt"], NT * NPT).rearrange("p (t n) -> p t n", t=NT)
        xbT = region(place["xb"], NXB * TOK).rearrange("p (b t) -> p b t", b=NXB)
        xBtok = region(place["xb"], NT * 512).rearrange("p (t n) -> p t n", t=NT)
        cvT = region(place["cv"], NXB * TOK).rearrange("p (b t) -> p b t", b=NXB)
        con = region(place["con"], NCONST)
        sw = region(place["sw"], NSW)
        wuq = sw[:, 0:768].rearrange("p (k n) -> p k n", k=2)
        wuk, wuv = sw[:, 768:1024], sw[:, 1024:1280]
        wg = sw[0:32, 1280:1536].rearrange("p (d n) -> p d n", d=2)
        col = region(place["col"], NCOL)
        row = region(place["row"], NROW)
        lnr = region(place["ln"], 4 * D).rearrange("p (r n) -> p r n", r=4)

        def C(name):
            a, n = CONST[name]
            return con[:, a:a + n]

        def scratch(base, n, tensor=arena, parts=P):
            return tensor[0:parts, base:base + n]

        def split(ap, **kw):
            names = " ".join(kw)
            return ap.rearrange(f"p ({names}) -> p {names}", **{k: v for k, v in kw.items()})

        def spread(ap, shape, axis):
            return ap.unsqueeze(axis).to_broadcast(shape)

        cqT = split(scratch(XM, 1024), k=2, t=TOK)
        ckvT = scratch(XM + 1024, 512)
        vtok = split(scratch(XM + 1536, 1024), t=NT, n=GW)
        probs = split(scratch(XM + 2560, 1024), s=2, n=512)
        qtok = split(scratch(0, 1536, rows3), t=NT, h=HEADS, n=QKD)
        ktok = split(scratch(1536, 1536, rows3), t=NT, h=HEADS, n=QKD)
        qT = split(scratch(W2, 2048), h=HEADS, t=TOK)
        kT = split(scratch(W2 + 2048, 2048), h=HEADS, t=TOK)
        pT = split(scratch(0, 1024, xT), s=2, n=512)
        ropeA = split(scratch(1024, 512, xT), t=NT, h=HEADS, n=ROPE)
        ropeB = split(scratch(1536, 512, xT), t=NT, h=HEADS, n=ROPE)
        gz = scratch(XM, 1024)
        ge = scratch(XM + 1024, 1024)
        gc = scratch(XM + 2048, 1024)
        lrT = scratch(XM + 3072, 512)
        gqT = scratch(XM + 3584, 512)
        gkT = scratch(W2, 512)
        gE1 = scratch(W2 + 512, 1024)
        gE2 = scratch(W2 + 1536, 1024)
        gKtok = split(scratch(W2 + 2560, 1024), d=2, t=NT, n=P)
        gQx = split(scratch(W2 + 3584, 1024), d=2, h=HEADS, i=P)
        states = split(scratch(0, 2048, xT), d=2, t=NT, n=GW)
        mats = split(scratch(0, 2048, rows3), s=2, d=2, n=512)
        work = split(scratch(2048, 1024, rows3), s=4, n=GW)
        rA = split(scratch(XM, 1024), t=NT, h=8, n=DK)
        rB = split(scratch(XM + 1024, 1024), t=NT, h=8, n=DK)
        rqT = split(scratch(XM + 2048, 512), t=NT, n=P)
        rkT = split(scratch(XM + 2560, 512), t=NT, n=P)
        rQ = split(scratch(XM + 3072, 1024), d=2, t=NT, n=P)
        rV = split(scratch(W2, 2048), d=2, t=NT, n=GW)
        rQx = split(scratch(W2 + 2048, 1024), s=2, h=HEADS, i=P)
        sm = scratch(XM, 512)
        s_dt, s_la, s_cum, s_w, s_el, s_t = (split(sm[:, 32 * i:32 * i + 32], t=NT, n=8) for i in range(6))
        laM = split(scratch(XM + 512, 1024), d=2, h=HEADS, i=P)
        sD = split(scratch(XM + 1536, 1024), d=2, h=HEADS, i=P)
        sE = split(scratch(XM + 2560, 1024), d=2, h=HEADS, i=P)
        sQ = split(scratch(W2, 1024), d=2, h=HEADS, i=P)
        sV = split(scratch(W2 + 1024, 2048), d=2, t=NT, n=GW)
        sM = split(scratch(W2 + 3072, 1024), d=2, n=512)
        sVw = split(scratch(0, 2048, rows3), d=2, t=NT, n=GW)
        norm_sq = split(scratch(XM, 1024), t=NT, n=GW)
        vals = split(scratch(0, 512), t=2, b=16, n=16)
        idxu = split(scratch(512, 512).bitcast(U32), t=2, b=16, n=16)
        idxf = split(scratch(1024, 512), t=2, b=16, n=16)
        cand = split(scratch(1536, 2048), h=PH, n=256)
        ctmp = scratch(3584, 256)
        vsel = split(scratch(3840, 256), t=2, h=PH, n=16)
        cidx = scratch(4096, 256).bitcast(U32)
        cidxu = split(cidx, t=2, h=PH, n=16)
        cab = scratch(4352, 512).bitcast(U32)
        cabf = scratch(4864, 512)
        eq = split(scratch(5376, 2048), h=PH, k=16, a=16)
        sel = split(scratch(7424, 768), w=3, t=2, n=P)
        gates = split(scratch(0, 32768), t=256, i=P)
        xTk = split(scratch(10240, 2048), k=KD, t=256)
        xs2 = split(scratch(12288, 2048), t=2, n=D)
        hotJ = split(scratch(6144, 1024, flat), s=2, u=4, n=P)
        hotI = split(scratch(7168, 1024, flat), s=2, u=4, n=P)
        xs3 = split(scratch(0, 2048), t=2, n=D)
        grow = split(scratch(2048, 3072), r=3, n=D)

        class Count:

            def __init__(self, eng, own):
                self.eng, self.own, self.n = eng, own, {}

            def up(self, name, n=1):
                self.n[name] = self.n.get(name, 0) + n
                return self.n[name]

            def step(self, ins):
                ins.then_inc(S(self.own), 1)
                self.eng.wait_ge(S(self.own), self.up(self.own))

            def tell(self, name):
                self.eng.sem_inc(S(name), 1)
                self.up(name)

            def await_(self, name, n=1):
                self.eng.wait_ge(S(name), self.up(name, n))

        class Filler:

            def __init__(self, who, first):
                self.who, self.first, self.n = who, first, 0

            def open(self, pe):
                if self.n >= 4:
                    pe.wait_ge(S(f"{self.who}_emptied"), self.n - 3)
                self.n += 1
                return bank[self.first + (self.n - 1) % 4]

            def close(self, ins):
                ins.then_inc(S(f"{self.who}_filled"), 1)

            def flushed(self, pe):
                pe.wait_ge(S(f"{self.who}_filled"), self.n)

            def settled(self, pe):
                if self.n:
                    pe.wait_ge(S(f"{self.who}_emptied"), self.n)

        class Emptier:
            def __init__(self, who, first, eng):
                self.who, self.first, self.n, self.eng = who, first, 0, eng

            def take(self):
                self.eng.wait_ge(S(f"{self.who}_filled"), self.n + 1)
                self.n += 1
                return bank[self.first + (self.n - 1) % 4]

            def free(self, ins):
                ins.then_inc(S(f"{self.who}_emptied"), 1)
                self.eng.wait_ge(S(f"{self.who}_emptied"), self.n)

        SWEEPS = [(0, 0), (0, 1), (1, 1)]

        def first_tile(L):
            return 0 if L < DEPTH - 1 else NT // 2

        ORDER = ((0, 1, 2, 3), (1, 0, 3, 2))

        def use(load, slot):
            return 16 * (load // 2 + 1)

        block = ctx.enter_context(nc.Block())

        @block.sync
        def _(sp):
            n = [0]

            def chunk(src):
                k = n[0]
                if k >= 2:
                    sp.wait_ge(S("chunk_used"), k - 1)
                sp.dma_start(stream[:, k % 2, :], src).then_inc(S(f"chunk_in{k % 2}"), 16)
                n[0] += 1

            for c in range(2):
                chunk(A["wada"][c])
            with sp.Fori(1, DEPTH * NADA // 2) as i:
                for c in range(2):
                    sp.wait_ge(S("chunk_used"), 2 * i + c - 1)
                    sp.dma_start(stream[:, c, :], A["wada"][2 * i + c]).then_inc(S(f"chunk_in{c}"), 16)
            n[0] = DEPTH * NADA
            sweep = 0
            for L in range(DEPTH):
                for c in range(NWIN):
                    chunk(A["win"][L * NWIN + c])
                for c in range(NWOUT):
                    chunk(A["wout"][L * NWOUT + c])
                for _ in range(len([x for x in SWEEPS if x[0] == L])):
                    for c in range(NWQ):
                        chunk(A["wq"][L * NWQ + c])
                    base = sweep * BLOCKS
                    sp.wait_ge(S("x_saved"), 16 * (1, 2, 4)[sweep])

                    def expert_block(n, sl, first):
                        for w, name in enumerate("uv"):
                            if not first:
                                sp.wait_ge(S(f"{name}_split"), base + n - 1)
                            sp.dma_start(raw[:, w, sl, :], A[name][L * BLOCKS + n]).then_inc(S(f"{name}_in{sl}"), 16)

                    expert_block(0, 0, True)
                    expert_block(1, 1, True)
                    with sp.Fori(1, BLOCKS // 2) as i:
                        expert_block(2 * i, 0, False)
                        expert_block(2 * i + 1, 1, False)
                    sp.wait_ge(S("experts_summed"), base + BLOCKS)
                    sweep += 1
            sp.wait_ge(S("normed"), 5)
            for t in range(NT // 2, NT):
                sp.dma_start(out[0, (t - 2) * P:(t - 1) * P, :], xs3[:, t - 2, :]).then_inc(S("out_stored"), 16)
            sp.wait_ge(S("out_stored"), 32)

        @block.gpsimd
        def _(pool):
            c = Count(pool, "pool_step")
            pool.dma_start(iota[:, :], A["iota"]).then_inc(S("base_in"), 16)
            pool.dma_start(ident[:, :], A["ident"]).then_inc(S("base_in"), 16)
            for t in range(NT):
                src = A["ctx"][0] if t < 2 else A["x"][0]
                pool.dma_start(X[:, t, :], src[(t % 2) * P:(t % 2 + 1) * P, :]).then_inc(S("base_in"), 16)
            pool.dma_start(small[:, 0:8], A["c_cols"]).then_inc(S("cond_in"), 16)
            pool.dma_start(small[:, 8:16], A["cctx_cols"]).then_inc(S("cond_in"), 16)
            pool.dma_start(arena[0:2, 0:DEPTH * 6 * D], A["b_ada"].rearrange("l n -> (l n)").partition_broadcast(2)).then_inc(S("cond_in"), 16)
            with pool.Fori(0, DEPTH * NADA // 4) as i:
                for u in range(4):
                    pool.wait_ge(S("mod_made"), 4 * i + u + 1)
                    pool.dma_start(modd.rearrange("s l (c n) -> s (l c) n", n=512)[:, 4 * i + u, :],
                                   arena[0:2, 16384 + 512 * u:16384 + 512 * (u + 1)]).then_inc(S(f"mod_stored{u}"), 16)
            for u in range(4):
                pool.wait_ge(S(f"mod_stored{u}"), 16 * DEPTH * NADA // 4)
            for L in range(DEPTH):
                if L:
                    pool.wait_ge(S("normed"), 3)
                    pool.wait_ge(S("x_saved"), 16 * 3)
                    pool.dma_start(X[:, :, :], xd.rearrange("t p n -> p t n")).then_inc(S("x_back"), 16)
                for r in range(2):
                    pool.dma_start(arena[48 * r:48 * r + 48, place["xb"]:place["xb"] + P],
                                   modd[r, L].rearrange("(v p) -> v p", p=P)).then_inc(S("modrow_in"), 16)
                pool.dma_start(con, A["const"]).then_inc(S("params_in"), 16)
                pool.dma_start(sw, A["smallw"][L]).then_inc(S("params_in"), 16)
                pool.dma_start(col, A["cols"][L]).then_inc(S("params_in"), 16)
                pool.dma_start(row, A["rows"][L].partition_broadcast(P)).then_inc(S("params_in"), 16)
                pool.dma_start(keysT[:, :, :], A["keys"][L]).then_inc(S("params_in"), 16)
                for r in range(2):
                    pool.dma_start(lnr[:, r, :], A["ln"][L, r].partition_broadcast(P)).then_inc(S("params_in"), 16)
                    pool.dma_start(lnr[:, 2 + r, :], modd[r, L, 2 * D:3 * D].partition_broadcast(P)).then_inc(S("params_in"), 16)
                pool.wait_ge(S("normed"), 1 if L == 0 else 4)
                pool.dma_start(xd.rearrange("t p n -> p t n"), X[:, :, :]).then_inc(S("x_saved"), 16)
                saved = 1 if L == 0 else 4
                for s, (LL, g) in enumerate(SWEEPS):
                    if LL != L:
                        continue
                    pool.wait_ge(S("x_saved"), 16 * saved)
                    pool.dma_start(xs2, xd[2 * g:2 * g + 2].rearrange("t p n -> p t n")).then_inc(S("tiles_in"), 16)
                    pool.wait_ge(S("act_weighed"), BLOCKS * (s + 1))
                    pool.dma_start(xs3, xd[2 * g:2 * g + 2].rearrange("t p n -> p t n")).then_inc(S("rows_in"), 16)
                    pool.dma_start(grow[:, 0, :], modd[g, L, 5 * D:6 * D].partition_broadcast(P)).then_inc(S("rows_in"), 16)
                    pool.dma_start(grow[:, 1, :], A["ln"][L, 2].partition_broadcast(P)).then_inc(S("rows_in"), 16)
                    pool.dma_start(grow[:, 2, :], A["ln"][L, 3].partition_broadcast(P)).then_inc(S("rows_in"), 16)
                    if L < DEPTH - 1:
                        pool.wait_ge(S("normed"), 2 + s)
                        pool.dma_start(xd[2 * g:2 * g + 2].rearrange("t p n -> p t n"), xs3).then_inc(S("x_saved"), 16)
                        saved += 1

        @block.tensor
        def _(pe):
            c = Count(pe, "pe_step")
            toA, toV = Filler("act", 0), Filler("dve", 4)
            chunks = [0]

            def mm(o, lhsT, rhs, start=True, stop=True):
                return nc.tensor.matmul(o, lhsT, rhs, start=start, stop=stop, skip_group_check=True)

            def tr(o, i):
                return nc.tensor.transpose(o, i, ident[0:i.shape[0], 0:i.shape[0]])

            def chunk_ready():
                k = chunks[0]
                pe.wait_ge(S(f"chunk_in{k % 2}"), use(k, k % 2))
                return split(stream[:, k % 2, :], k=KD, n=512)

            def chunk_done():
                chunks[0] += 1

            def settle():
                toA.settled(pe)
                toV.settled(pe)

            pe.wait_ge(S("base_in"), 16 * 6)
            pe.wait_ge(S("cond_ready"), 1)
            cs = split(small[:, 16:32], s=2, k=KD)

            def ada(i, u, first):
                pe.wait_ge(S(f"chunk_in{u % 2}"), 32 * i + 16 * (u // 2 + 1))
                if not first:
                    pe.wait_ge(S("mod_made"), 4 * i + u - 3)
                w = split(stream[:, u % 2, :], k=KD, n=512)
                for k in range(KD):
                    m = mm(bank[4 + u][0:2, :], cs[:, :, k], w[:, k, :], k == 0, k == KD - 1)
                m.then_inc(S("chunk_used"), 1)

            for u in range(4):
                ada(0, u, True)
            with pe.Fori(1, DEPTH * NADA // 4) as i:
                for u in range(4):
                    ada(i, u, False)
            pe.wait_ge(S("mod_made"), DEPTH * NADA)
            chunks[0] = DEPTH * NADA

            def mixers(L):
                T0 = first_tile(L)
                c.await_("modrow_in", 32)
                b = toV.open(pe)
                toV.close(tr(b[:, 0:96], arena[0:96, place["xb"]:place["xb"] + P]))
                c.await_("mod_columns")
                if L:
                    pe.wait_ge(S("x_back"), 16)
                for k in range(KD):
                    ring = toA if k % 2 == 0 else toV
                    b = ring.open(pe)
                    for t in range(NT):
                        m = tr(b[:, t * P:(t + 1) * P], X[:, t, k * P:(k + 1) * P])
                    ring.close(m)
                settle()
                unit = 0
                for ch in range(NWIN):
                    w = chunk_ready()
                    nb = {0: 4, 1: 2}.get(ch, 0)
                    for bl in range(nb):
                        ring = toA if unit % 2 == 0 else toV
                        unit += 1
                        b = ring.open(pe)
                        for k in range(KD):
                            m = mm(b[:, :], w[:, k, bl * P:(bl + 1) * P], xmT[:, k, :], k == 0, k == KD - 1)
                        ring.close(m)
                    lo = nb * P
                    hi = 512 if ch < NWIN - 1 else NPT - 256 - 3 * 512
                    for t in range(NT if lo < hi else 0):
                        ring = toA if unit % 2 == 0 else toV
                        unit += 1
                        b = ring.open(pe)
                        for k in range(KD):
                            m = mm(b[:, 0:hi - lo], xmT[:, k, t * P:(t + 1) * P], w[:, k, lo:hi], k == 0, k == KD - 1)
                        ring.close(m)
                    ring.flushed(pe)
                    pe.sem_inc(S("chunk_used"), 1)
                    chunk_done()

                pe.wait_ge(S("params_in"), 16 * 9 * (L + 1))
                c.await_("mla_latents")
                for k in range(2):
                    b = toA.open(pe)
                    for t in range(NT):
                        m = tr(b[:, t * P:(t + 1) * P], ptok[:, t, O_CQ + k * P:O_CQ + (k + 1) * P])
                    toA.close(m)
                b = toV.open(pe)
                for t in range(NT):
                    m = tr(b[:, t * P:(t + 1) * P], ptok[:, t, O_CKV:O_CKV + P])
                toV.close(m)
                settle()
                for t in range(NT):
                    b = toA.open(pe)
                    mm(b[:, 0:GW], ckvT[:, t * P:(t + 1) * P], wuk)
                    toA.close(mm(b[:, GW:2 * GW], ckvT[:, t * P:(t + 1) * P], wuv))
                    if t >= T0:
                        b = toV.open(pe)
                        for k in range(2):
                            m = mm(b[:, 0:HEADS * QKD], cqT[:, k, t * P:(t + 1) * P], wuq[:, k, :], k == 0, k == 1)
                        toV.close(m)
                c.await_("mla_rotated")
                for h in range(HEADS):
                    b = toA.open(pe)
                    for t in range(NT):
                        m = tr(b[0:QKD, t * P:(t + 1) * P], ktok[:, t, h, :])
                    toA.close(m)
                    b = toV.open(pe)
                    for t in range(T0, NT):
                        m = tr(b[0:QKD, t * P:(t + 1) * P], qtok[:, t, h, :])
                    toV.close(m)
                settle()
                units = [(t, h) for t in range(T0, NT) for h in range(HEADS)]
                ub = 16 * L

                def keys_of(t):
                    return CTX if t < 2 else TOK

                def scores(i):
                    t, h = units[i]
                    if i >= 2:
                        pe.wait_ge(S("probs_ready"), ub + i - 1)
                    mm(bank[i % 2][:, 0:keys_of(t)], qT[0:QKD, h, t * P:(t + 1) * P], kT[0:QKD, h, 0:keys_of(t)]
                       ).then_inc(S("scores_filled"), 1)

                def turn(i):
                    pe.wait_ge(S("probs_ready"), ub + i + 1)
                    if i >= 2:
                        pe.wait_ge(S("turned_emptied"), ub + i - 1)
                    for j in range(keys_of(units[i][0]) // P):
                        m = tr(bank[2 + i % 2][:, j * P:(j + 1) * P], probs[:, i % 2, j * P:(j + 1) * P])
                    m.then_inc(S("turned_filled"), 1)

                def weigh(i):
                    t, h = units[i]
                    n = i // HEADS
                    nk = keys_of(t) // P
                    pe.wait_ge(S("turned_emptied"), ub + i + 1)
                    if h == 0 and n >= 2:
                        pe.wait_ge(S("tile_attended"), ub // HEADS + n - 1)
                    for j in range(nk):
                        m = mm(bank[4 + n % 2][:, h * VD:(h + 1) * VD], pT[:, i % 2, j * P:(j + 1) * P],
                               vtok[:, j, h * VD:(h + 1) * VD], j == 0, j == nk - 1)
                    m.then_inc(S("weighed"), 1)

                scores(0)
                scores(1)
                for i in range(len(units)):
                    turn(i)
                    if i + 2 < len(units):
                        scores(i + 2)
                    weigh(i)
                pe.wait_ge(S("tile_attended"), ub // HEADS + len(units) // HEADS)

                b = toV.open(pe)
                for t in range(NT):
                    m = tr(b[0:32, t * P:(t + 1) * P], ptok[:, t, O_GL:O_GL + 32])
                toV.close(m)
                for o in (O_GQ, O_GK):
                    b = toA.open(pe)
                    for t in range(NT):
                        m = tr(b[:, t * P:(t + 1) * P], ptok[:, t, o:o + P])
                    toA.close(m)
                settle()
                for d in range(2):
                    b = toA.open(pe)
                    toA.close(mm(b[:, :], wg[:, d, :], lrT[0:32, :]))
                c.await_("gla_scaled")
                for d in range(2):
                    b = toA.open(pe)
                    for t in range(NT):
                        m = tr(b[:, t * P:(t + 1) * P], gE2[:, d * TOK + t * P:d * TOK + (t + 1) * P])
                    toA.close(m)
                settle()
                scan_states("gla", lambda d, t: (gKtok[:, d, t, :], ptok[:, t, O_GV:O_GV + GW]))
                for n, t in enumerate(range(T0, NT)):
                    for d in range(2):
                        c.await_("gla_spread")
                        b = toV.open(pe)
                        toV.close(mm(b[:, :], gE2[:, d * TOK + t * P:d * TOK + (t + 1) * P], gQx[:, d, :, :]))
                    toV.settled(pe)
                    b = toA.open(pe)
                    first = True
                    for d in range(2):
                        if t != ORDER[d][0]:
                            m = mm(b[:, 0:GW], gE1[:, d * TOK + t * P:d * TOK + (t + 1) * P], states[:, d, t, :], first, False)
                            first = False
                    for h in range(HEADS):
                        for d in range(2):
                            m = mm(b[:, h * DV:(h + 1) * DV], mats[:, n % 2, d, h * P:(h + 1) * P],
                                   ptok[:, t, O_GV + h * DV:O_GV + (h + 1) * DV], first, d == 1)
                            first = False
                    toA.close(m)
                settle()

                c.await_("ret_rotated")
                for o in (O_RQ, O_RK):
                    b = toA.open(pe)
                    for t in range(NT):
                        m = tr(b[:, t * P:(t + 1) * P], ptok[:, t, o:o + P])
                    toA.close(m)
                settle()
                c.await_("ret_scaled")
                scan_states("ret", lambda d, t: (ptok[:, t, O_RK:O_RK + P], rV[:, d, t, :]))
                for n, t in enumerate(range(T0, NT)):
                    c.await_("ret_spread")
                    b = toV.open(pe)
                    toV.close(mm(b[:, :], rkT[:, t, :], rQx[:, n % 2, :, :]))
                    toV.settled(pe)
                    b = toA.open(pe)
                    first = True
                    for d in range(2):
                        if t != ORDER[d][0]:
                            m = mm(b[:, 0:GW], rQ[:, d, t, :], states[:, d, t, :], first, False)
                            first = False
                    for h in range(HEADS):
                        m = mm(b[:, h * DV:(h + 1) * DV], mats[:, n % 2, 0, h * P:(h + 1) * P],
                               ptok[:, t, O_RV + h * DV:O_RV + (h + 1) * DV], first, True)
                        first = False
                    toA.close(m)
                settle()

                c.await_("ssd_conv")
                for t in range(NT):
                    b = toA.open(pe)
                    for j in range(4):
                        m = tr(b[:, j * P:(j + 1) * P], cvT[:, j, t * P:(t + 1) * P])
                    toA.close(m)
                c.await_("ssd_rates")
                b = toV.open(pe)
                for t in range(NT):
                    for d, mask in enumerate(("maskF", "maskB")):
                        m = mm(b[:, t * 8 + 4 * d:t * 8 + 4 * d + 4], C(mask), s_la[:, t, 4 * d:4 * d + 4])
                toV.close(m)
                b = toV.open(pe)
                toV.close(mm(b[:, 0:32], C("ones"), sm[:, 32:64]))
                settle()
                c.await_("ssd_values")
                scan_states("ssd", None)
                for n, t in enumerate(range(T0, NT)):
                    for d in range(2):
                        c.await_("ssd_masked")
                        b = toV.open(pe)
                        toV.close(mm(b[:, :], C("ones"), laM[:, d, :, :]))
                    b = toV.open(pe)
                    for g in range(2):
                        m = mm(b[:, g * P:(g + 1) * P], cvT[:, 2 + g, t * P:(t + 1) * P], cvT[:, 4 + g, t * P:(t + 1) * P])
                    toV.close(m)
                    c.await_("ssd_decayed")
                    toV.settled(pe)
                    b = toA.open(pe)
                    first = True
                    for h in range(HEADS):
                        o = b[:, h * DV:(h + 1) * DV]
                        for d in range(2):
                            if t != ORDER[d][0]:
                                mm(o, sQ[:, d, h, :], states[:, d, t, h * DV:(h + 1) * DV], first, False)
                                first = False
                        for d in range(2):
                            m = mm(o, sM[:, d, h * P:(h + 1) * P], sV[:, d, t, h * DV:(h + 1) * DV], first, d == 1)
                            first = False
                    toA.close(m)
                settle()

                c.await_("mixed")
                for k in range(KD):
                    ring = toA if k % 2 == 0 else toV
                    o = (O_CQ, O_GQ, O_Z, O_RQ)[k // 2] + (k % 2) * P
                    b = ring.open(pe)
                    for t in range(T0, NT):
                        m = tr(b[:, t * P:(t + 1) * P], ptok[:, t, o:o + P])
                    ring.close(m)
                settle()
                for ch in range(NWOUT):
                    w = chunk_ready()
                    for t in range(T0, NT):
                        b = toV.open(pe)
                        for k in range(KD):
                            m = mm(b[:, :], xmT[:, k, t * P:(t + 1) * P], w[:, k, :], k == 0, k == KD - 1)
                        toV.close(m)
                    toV.flushed(pe)
                    pe.sem_inc(S("chunk_used"), 1)
                    chunk_done()

            def scan_states(kind, operands):
                for step in range(NT - 1):
                    for d in range(2):
                        t = ORDER[d][step]
                        b = toV.open(pe)
                        if operands:
                            k, v = operands(d, t)
                            m = mm(b[:, 0:GW], k, v)
                        else:
                            for g in range(2):
                                m = mm(b[:, g * P:(g + 1) * P], xBtok[:, t, 256 + g * P:256 + (g + 1) * P],
                                       sVw[:, d, t, g * P:(g + 1) * P])
                        toV.close(m)
                c.await_("states_ready")

            def experts(s, L, g):
                pe.wait_ge(S("tiles_in"), 16 * (s + 1))
                for k in range(KD):
                    ring = toA if k % 2 == 0 else toV
                    b = ring.open(pe)
                    for t in range(2):
                        m = tr(b[:, t * P:(t + 1) * P], xs2[:, t, k * P:(k + 1) * P])
                    ring.close(m)
                settle()

                def query(bl):
                    w = split(stream[:, chunks[0] % 2, :], k=KD, n=512)
                    b = toA.open(pe)
                    for k in range(KD):
                        m = mm(b[:, 0:256], w[:, k, (bl % 4) * P:(bl % 4 + 1) * P], xTk[:, k, :], k == 0, k == KD - 1)
                    toA.close(m)

                def key_scores(bl):
                    toA.settled(pe)
                    b = toV.open(pe)
                    for t in range(2):
                        m = mm(b[:, t * P:(t + 1) * P], acts[:, bl % 2, t * P:(t + 1) * P], keysT[:, bl % 2, :])
                    toV.close(m)

                for ch in range(NWQ):
                    chunk_ready()
                    for i in range(4):
                        query(4 * ch + i)
                        key_scores(4 * ch + i)
                    toV.flushed(pe)
                    pe.sem_inc(S("chunk_used"), 1)
                    chunk_done()
                c.await_("picked")
                for w in range(3):
                    b = toV.open(pe)
                    for t in range(2):
                        m = tr(b[:, t * P:(t + 1) * P], sel[:, w, t, :])
                    toV.close(m)
                settle()
                gbase = 64 * s

                def tokens(i, u):
                    n = gbase + 4 * i + u
                    pe.wait_ge(S("hots_ready"), n + 1)
                    if not isinstance(n, int) or n >= 4:
                        pe.wait_ge(S("gates_emptied"), n - 3)
                    for q in range(4):
                        m = mm(bank[u][:, q * P:(q + 1) * P], hotJ[:, u % 2, q, :], hotI[:, u % 2, q, :])
                    m.then_inc(S("gates_filled"), 1)

                for u in range(4):
                    tokens(0, u)
                with pe.Fori(1, 16) as i:
                    for u in range(4):
                        tokens(i, u)
                pe.wait_ge(S("gates_emptied"), gbase + 64)
                base = BLOCKS * s
                outb = [toV.open(pe) for _ in range(4)]
                parts = ((0, 0), (0, 1), (1, 0))

                def hidden(n, sl):
                    pe.wait_ge(S("u_split"), base + n + 1)
                    if not isinstance(n, int) or n >= 2:
                        pe.wait_ge(S("gelu_done"), base + n - 1)
                    for k in range(KD):
                        for a, b in parts:
                            m = mm(bank[sl][:, 0:256], splits[:, sl, a, k * P:(k + 1) * P], xTr[:, b, k, :],
                                   k == 0 and a + b == 0, k == KD - 1 and a == 1)
                    m.then_inc(S("hidden_filled"), 1)

                def summed(n, sl, first=False, last=False):
                    pe.wait_ge(S("v_split"), base + n + 1)
                    pe.wait_ge(S("act_ready"), base + n + 1)
                    for t in range(2):
                        for hf in range(2):
                            for a, b in parts:
                                m = mm(outb[2 * t + hf][:, :], actr[:, sl, a, t * P:(t + 1) * P],
                                       splits[:, 2 + sl, b, hf * 512:(hf + 1) * 512], first and a + b == 0, last and a == 1)
                    m.then_inc(S("experts_summed"), 1)

                pe.wait_ge(S("x_split"), s + 1)
                hidden(0, 0)
                hidden(1, 1)
                summed(0, 0, first=True)
                hidden(2, 0)
                summed(1, 1)
                with pe.Fori(1, BLOCKS // 2 - 1) as i:
                    hidden(2 * i + 1, 1)
                    summed(2 * i, 0)
                    hidden(2 * i + 2, 0)
                    summed(2 * i + 1, 1)
                hidden(BLOCKS - 1, 1)
                summed(BLOCKS - 2, 0)
                summed(BLOCKS - 1, 1, last=True)
                pe.wait_ge(S("experts_summed"), base + BLOCKS)
                pe.sem_inc(S("dve_filled"), 4)

            s = 0
            for L in range(DEPTH):
                mixers(L)
                while s < len(SWEEPS) and SWEEPS[s][0] == L:
                    experts(s, *SWEEPS[s])
                    s += 1

        @block.scalar
        def _(act):
            c = Count(act, "act_step")
            ring = Emptier("act", 0, act)
            go = nc.scalar.activation

            act.wait_ge(S("cond_in"), 48)
            c.step(go(small[:, 16:24], small[:, 8:16], ACT.Silu))
            c.step(go(small[:, 24:32], small[:, 0:8], ACT.Silu))
            c.tell("cond_ready")

            def modulated(dst, b, k, s, a, n, v, last):
                ins = go(dst, b[:, a:a + n], ACT.Identity, bias=modc[:, s, v, k:k + 1], scale=modc[:, s, v + 1, k:k + 1])
                if last:
                    ring.free(ins)

            def norm_scale(src, dst, name):
                c.await_(name)
                c.step(go(dst, src, ACT.Ln))
                c.step(go(dst, dst, ACT.Exp, scale=-0.5))
                c.tell(name + "_root")

            def mixers(L):
                T0 = first_tile(L)
                TS = slice(T0, NT)
                c.await_("mod_columns")
                for k in range(0, KD, 2):
                    b = ring.take()
                    modulated(xmT[:, k, 0:CTX], b, k, 0, 0, CTX, 0, False)
                    modulated(xmT[:, k, CTX:TOK], b, k, 1, CTX, SEQ, 0, True)
                units = [("x", b) for b in range(NXB)] + [("t", ch, t) for ch in range(1, NWIN) for t in range(NT)]
                for u in units[::2]:
                    b = ring.take()
                    if u[0] == "x":
                        ring.free(go(xbT[:, u[1], :], b[:, :], ACT.Copy))
                    else:
                        ch, t = u[1:]
                        a = 0 if ch == 1 else 256 + (ch - 2) * 512
                        n = 256 if ch == 1 else min(512, NPT - a)
                        ring.free(go(ptok[:, t, a:a + n], b[:, 0:n], ACT.Copy))
                c.tell("projected_by_act")
                c.await_("projected_by_dve")
                for o in (O_GR, O_Z, O_RG):
                    c.step(go(ptok[:, TS, o:o + GW], ptok[:, TS, o:o + GW], ACT.Silu))
                c.await_("conv_summed")
                c.step(go(cvT[:, :, :], cvT[:, :, :], ACT.Silu))
                c.tell("ssd_conv")
                act.wait_ge(S("params_in"), 16 * 9 * (L + 1))
                for t in range(NT):
                    c.step(go(cqT[:, 0, 0:QLORA], ptok[:, t, O_CQ:O_CQ + QLORA], ACT.Square, accum_out=small[:, 40 + t:41 + t]))
                    c.step(go(cqT[:, 0, 0:KVLORA], ptok[:, t, O_CKV:O_CKV + KVLORA], ACT.Square, accum_out=small[:, 44 + t:45 + t]))
                c.tell("latent_squares")
                norm_scale(small[:, 32:40], small[:, 40:48], "latent_meansq")
                for k in range(2):
                    b = ring.take()
                    ring.free(go(cqT[:, k, :], b[:, :], ACT.Copy, scale=col[:, C_GQ + k:C_GQ + k + 1]))
                for t in range(NT):
                    b = ring.take()
                    go(ktok[:, t, :, 0:NOPE], split(b[:, 0:GW], h=HEADS, n=NOPE), ACT.Copy)
                    ring.free(go(vtok[:, t, :], b[:, GW:2 * GW], ACT.Copy))
                c.tell("mla_keys")
                for h in range(HEADS):
                    b = ring.take()
                    ring.free(go(kT[0:QKD, h, :], b[0:QKD, :], ACT.Copy))
                units = [(t, h) for t in range(T0, NT) for h in range(HEADS)]
                for i, (t, h) in enumerate(units):
                    nk = CTX if t < 2 else TOK
                    act.wait_ge(S("row_max"), 16 * L + i + 1)
                    if i >= 2:
                        act.wait_ge(S("turned_filled"), 16 * L + i - 1)
                    go(probs[:, i % 2, 0:nk], bank[i % 2][:, 0:nk], ACT.Exp, bias=small[:, 64 + i:65 + i],
                       accum_out=small[:, 48 + i:49 + i]).then_inc(S("probs_ready"), 1)

                b = ring.take()
                ring.free(go(gqT, b[:, :], ACT.Copy, scale=DK ** -0.5))
                b = ring.take()
                ring.free(go(gkT, b[:, :], ACT.Copy))
                for d in range(2):
                    b = ring.take()
                    ring.free(go(gz[:, d * TOK:(d + 1) * TOK], b[:, :], ACT.Identity, bias=col[:, C_BGF + d:C_BGF + d + 1]))
                c.step(go(ge, gz, ACT.Abs))
                c.step(go(ge, ge, ACT.Exp, scale=-1.0))
                c.step(go(ge, ge, ACT.Ln, bias=1.0))
                c.tell("gla_logs")
                c.await_("gla_cums")
                c.step(go(gE1, ge, ACT.Exp, scale=1.0 / 16))
                c.step(go(gE2, ge, ACT.Exp, scale=-1.0 / 16))
                c.step(go(small[:, 112:136], small[:, 112:136], ACT.Exp, scale=1.0 / 16))
                c.tell("gla_exps")
                for d in range(2):
                    b = ring.take()
                    ring.free(go(gKtok[:, d, :, :], split(b[:, :], t=NT, n=P), ACT.Copy))
                for t in range(T0, NT):
                    b = ring.take()
                    ring.free(go(ptok[:, t, O_GQ:O_GQ + GW], b[:, 0:GW], ACT.Copy))
                c.tell("gla_outs")
                norm_scale(small[:, 80:96], small[:, 96:112], "gla_meansq")

                b = ring.take()
                ring.free(go(rqT, split(b[:, :], t=NT, n=P), ACT.Copy, scale=DK ** -0.5))
                b = ring.take()
                ring.free(go(rkT, split(b[:, :], t=NT, n=P), ACT.Copy))
                c.tell("ret_turned")
                for t in range(T0, NT):
                    b = ring.take()
                    ring.free(go(ptok[:, t, O_RQ:O_RQ + GW], b[:, 0:GW], ACT.Copy))
                c.tell("ret_outs")
                norm_scale(small[:, 80:96], small[:, 96:112], "ret_meansq")

                for t in range(NT):
                    b = ring.take()
                    ring.free(go(xBtok[:, t, :], b[:, :], ACT.Copy))
                c.await_("ssd_rates_raw")
                c.step(go(s_t, s_dt, ACT.Abs))
                c.step(go(s_t, s_t, ACT.Exp, scale=-1.0))
                c.step(go(s_t, s_t, ACT.Ln, bias=1.0))
                c.step(go(small[:, 136:144], row[:, R_ALOG:R_ALOG + 8], ACT.Exp))
                c.tell("ssd_logs")
                c.await_("ssd_sums")
                c.step(go(s_w, s_w, ACT.Exp))
                c.step(go(s_el, s_t, ACT.Exp))
                c.tell("ssd_decays")
                for t in range(T0, NT):
                    c.await_("ssd_exponents")
                    c.step(go(sE, sE, ACT.Exp))
                    c.step(go(sD, sD, ACT.Exp))
                    c.tell("ssd_exps")
                    b = ring.take()
                    ring.free(go(sVw[:, 0, t, :], b[:, 0:GW], ACT.Copy))
                c.tell("ssd_outs")
                norm_scale(small[:, 80:84], small[:, 96:100], "ssd_meansq")

                for k in range(0, KD, 2):
                    b = ring.take()
                    ring.free(go(xmT[:, k, T0 * P:TOK], b[:, T0 * P:TOK], ACT.Copy))
                norm_scale(small[:, 132:136], small[:, 136:140], "ln_var")

            def experts(s, L, g):
                for k in range(0, KD, 2):
                    b = ring.take()
                    modulated(xTk[:, k, :], b, k, g, 0, 256, 3, True)
                c.await_("x_modulated")
                go(xTr[:, 0, :, :], xTk, ACT.Copy).then_inc(S("x_high"), 1)
                for bl in range(2 * PH):
                    b = ring.take()
                    if bl >= 2:
                        act.wait_ge(S("query_used"), 2 * PH * s + bl - 1)
                    ring.free(go(acts[:, bl % 2, :], b[:, 0:256], ACT.Copy))
                c.await_("softmax_shifted")
                c.step(go(vsel, vsel, ACT.Exp))
                c.tell("softmax_exps")
                base = BLOCKS * s

                def high(name, n, sl, w, used):
                    act.wait_ge(S(f"{name}_in{sl}"), 16 * (BLOCKS // 2) * s + 8 * (n - sl) + 16)
                    if used is not None:
                        act.wait_ge(S(used), base + n - 1)
                    go(splits[:, 2 * w + sl, 0, :], raw[:, w, sl, :], ACT.Copy).then_inc(S(f"{name}_high"), 1)

                high("u", 0, 0, 0, None)
                high("u", 1, 1, 0, None)
                high("v", 0, 0, 1, None)
                gb = 64 * s

                def empty_gates(i, u):
                    n = gb + 4 * i + u
                    act.wait_ge(S("gates_filled"), n + 1)
                    go(gates[:, bass.ds(16 * i + 4 * u, 4), :], split(bank[u][:, :], t=4, i=P), ACT.Copy).then_inc(S("gates_emptied"), 1)

                with act.Fori(0, 16) as i:
                    for u in range(4):
                        empty_gates(i, u)

                def block_work(n, sl, more_u, more_v):
                    act.wait_ge(S("hidden_filled"), base + n + 1)
                    if not isinstance(n, int) or n >= 2:
                        act.wait_ge(S("act_ready"), base + n - 1)
                    go(acts[:, sl, :], bank[sl][:, 0:256], ACT.Gelu).then_inc(S("gelu_done"), 1)
                    act.wait_ge(S("act_weighed"), base + n + 1)
                    if not isinstance(n, int) or n >= 2:
                        act.wait_ge(S("experts_summed"), base + n - 1)
                    go(actr[:, sl, 0, :], acts[:, sl, :], ACT.Copy).then_inc(S("act_high"), 1)
                    if more_u:
                        high("u", n + 2, sl, 0, "hidden_filled")
                    if more_v:
                        high("v", n + 1, 1 - sl, 1, None if isinstance(n, int) and n == 0 else "experts_summed")

                block_work(0, 0, True, True)
                block_work(1, 1, True, True)
                with act.Fori(1, BLOCKS // 2 - 1) as i:
                    block_work(2 * i, 0, True, True)
                    block_work(2 * i + 1, 1, True, True)
                block_work(BLOCKS - 2, 0, False, True)
                block_work(BLOCKS - 1, 1, False, False)
                norm_scale(small[:, 132:134], small[:, 136:138], "ln_var")

            s = 0
            for L in range(DEPTH):
                mixers(L)
                while s < len(SWEEPS) and SWEEPS[s][0] == L:
                    experts(s, *SWEEPS[s])
                    s += 1

        @block.vector
        def _(dve):
            c = Count(dve, "dve_step")
            ring = Emptier("dve", 4, dve)
            V = nc.vector

            def tt(o, a, b, op):
                return V.tensor_tensor(o, a, b, op)

            def refined(v, r, n):
                w = small[:, 144:144 + n]
                c.step(tt(w, v, r, ALU.mult))
                c.step(tt(w, w, r, ALU.mult))
                c.step(V.tensor_scalar(w, w, -0.5, 1.5, ALU.mult, ALU.add))
                c.step(tt(r, r, w, ALU.mult))

            def layer_norm(x_of, tiles, b_rows, products, gate_of, g_row):
                for t, hf in products:
                    x = x_of(t)[:, hf * 512:(hf + 1) * 512]
                    b = ring.take()
                    tmp = b_rows
                    ins = tt(tmp, b[:, :], gate_of(t)[:, hf * 512:(hf + 1) * 512], ALU.mult)
                    ring.free(ins)
                    c.step(V.scalar_tensor_tensor(x, x, ALPHA, tmp, ALU.mult, ALU.add))
                for n, t in enumerate(tiles):
                    for hf in range(2):
                        c.step(V.bn_stats(small[:, 112 + 6 * hf:118 + 6 * hf], x_of(t)[:, hf * 512:(hf + 1) * 512]))
                    c.step(V.bn_aggr(small[:, 124 + 2 * n:126 + 2 * n], small[:, 112:124]))
                    c.step(V.tensor_scalar(small[:, 132 + n:133 + n], small[:, 125 + 2 * n:126 + 2 * n], 1e-5, None, ALU.add))
                c.tell("ln_var")
                c.await_("ln_var_root")
                refined(small[:, 132:132 + len(tiles)], small[:, 136:136 + len(tiles)], len(tiles))
                for n, t in enumerate(tiles):
                    c.step(V.tensor_scalar(x_of(t)[:, :], x_of(t)[:, :], small[:, 124 + 2 * n:125 + 2 * n], small[:, 136 + n:137 + n],
                                           ALU.subtract, ALU.mult))
                for r, op in enumerate((ALU.mult, ALU.add)):
                    for t in tiles:
                        c.step(tt(x_of(t)[:, :], x_of(t)[:, :], g_row(r), op))
                c.tell("normed")

            def ada(i, u, first):
                dve.wait_ge(S("chunk_used"), 4 * i + u + 1)
                if not first:
                    dve.wait_ge(S(f"mod_stored{u}"), 16 * i)
                tt(arena[0:2, 16384 + 512 * u:16384 + 512 * (u + 1)], bank[4 + u][0:2, :],
                   arena[0:2, bass.ds(2048 * i + 512 * u, 512)], ALU.add).then_inc(S("mod_made"), 1)

            dve.wait_ge(S("cond_in"), 48)
            for u in range(4):
                ada(0, u, True)
            with dve.Fori(1, DEPTH * NADA // 4) as i:
                for u in range(4):
                    ada(i, u, False)

            def modulated(dst, b, k, s, a, n, v, last):
                ins = V.tensor_scalar(dst, b[:, a:a + n], modc[:, s, v + 1, k:k + 1], modc[:, s, v, k:k + 1], ALU.mult, ALU.add)
                if last:
                    ring.free(ins)

            def head_scale(o, T0, centre, g_row, gate, name):
                n = NT - T0
                x = ptok[:, T0:NT, o:o + GW]
                heads = n * HEADS

                def by_head(ap):
                    return ap.rearrange("p t (h v) -> p t h v", h=HEADS)

                stat = small[:, 80:80 + heads]
                stat4 = split(stat, t=n, h=HEADS)
                shape = [P, n, HEADS, DV]
                sq = norm_sq[:, T0:NT, :]
                if centre:
                    c.step(V.tensor_reduce(stat4, by_head(x), AX.X, ALU.add))
                    c.step(V.tensor_scalar(stat, stat, 1.0 / DV, None, ALU.mult))
                    c.step(tt(by_head(x), by_head(x), spread(stat4, shape, 3), ALU.subtract))
                c.step(tt(sq, x, x, ALU.mult))
                c.step(V.tensor_reduce(stat4, by_head(sq), AX.X, ALU.add))
                c.step(V.tensor_scalar(small[:, 80:96], small[:, 80:96], 1.0 / DV, 1e-6, ALU.mult, ALU.add))
                c.tell(name)
                c.await_(name + "_root")
                refined(small[:, 80:96], small[:, 96:112], 16)
                c.step(tt(by_head(x), by_head(x), spread(split(small[:, 96:96 + heads], t=n, h=HEADS), shape, 3), ALU.mult))
                if g_row is not None:
                    c.step(tt(x, x, spread(g_row, [P, n, GW], 1), ALU.mult))
                c.step(tt(x, x, ptok[:, T0:NT, gate:gate + GW], ALU.mult))

            def mixers(L):
                T0 = first_tile(L)
                n_out = NT - T0
                b = ring.take()
                ring.free(V.tensor_copy(modc[:, :, :, :], split(b[:, 0:96], s=2, v=6, k=KD)))
                for v in (1, 4):
                    c.step(V.tensor_scalar(modc[:, :, v, :], modc[:, :, v, :], 1.0, None, ALU.add))
                if L == 0:
                    c.step(V.memset(small[:, 80:96], 1.0))
                c.tell("mod_columns")
                for k in range(1, KD, 2):
                    b = ring.take()
                    modulated(xmT[:, k, 0:CTX], b, k, 0, 0, CTX, 0, False)
                    modulated(xmT[:, k, CTX:TOK], b, k, 1, CTX, SEQ, 0, True)
                units = [("x", b) for b in range(NXB)] + [("t", ch, t) for ch in range(1, NWIN) for t in range(NT)]
                for u in units[1::2]:
                    b = ring.take()
                    if u[0] == "x":
                        ring.free(V.tensor_copy(xbT[:, u[1], :], b[:, :]))
                    else:
                        ch, t = u[1:]
                        a = 0 if ch == 1 else 256 + (ch - 2) * 512
                        n = 256 if ch == 1 else min(512, NPT - a)
                        ring.free(V.tensor_copy(ptok[:, t, a:a + n], b[:, 0:n]))
                c.tell("projected_by_dve")
                c.await_("projected_by_act")
                dve.wait_ge(S("params_in"), 16 * 9 * (L + 1))
                for bl in range(NXB):
                    w = [col[:, C_CW + 3 * bl + j:C_CW + 3 * bl + j + 1] for j in range(3)]
                    xs = split(xbT[:, bl, :], s=2, t=CTX)
                    ys = split(cvT[:, bl, :], s=2, t=CTX)
                    c.step(V.tensor_scalar(ys, xs, w[1], col[:, C_CB + bl:C_CB + bl + 1], ALU.mult, ALU.add))
                    c.step(V.scalar_tensor_tensor(ys[:, :, 1:CTX], xs[:, :, 0:CTX - 1], w[0], ys[:, :, 1:CTX], ALU.mult, ALU.add))
                    c.step(V.scalar_tensor_tensor(ys[:, :, 0:CTX - 1], xs[:, :, 1:CTX], w[2], ys[:, :, 0:CTX - 1], ALU.mult, ALU.add))
                c.tell("conv_summed")

                c.await_("latent_squares")
                c.step(V.tensor_scalar(small[:, 32:36], small[:, 40:44], 1.0 / QLORA, 1e-6, ALU.mult, ALU.add))
                c.step(V.tensor_scalar(small[:, 36:40], small[:, 44:48], 1.0 / KVLORA, 1e-6, ALU.mult, ALU.add))
                c.tell("latent_meansq")
                c.await_("latent_meansq_root")
                refined(small[:, 32:40], small[:, 40:48], 8)
                for t in range(NT):
                    for w, (o, n) in enumerate(((O_CQ, QLORA), (O_CKV, KVLORA))):
                        c.step(V.tensor_scalar(ptok[:, t, o:o + n], ptok[:, t, o:o + n], small[:, 40 + 4 * w + t:41 + 4 * w + t],
                                               None, ALU.mult))
                c.tell("mla_latents")
                kr = ptok[:, :, O_KR:O_KR + ROPE]
                cosA, sinA = split(C("cosA"), t=NT, n=ROPE), split(C("sinA"), t=NT, n=ROPE)
                hr = ROPE // 2
                c.step(tt(ropeA[:, :, 0, :], kr, cosA, ALU.mult))
                c.step(tt(ropeB[:, :, 0, :], kr, sinA, ALU.mult))
                for h in range(HEADS):
                    c.step(tt(ktok[:, :, h, NOPE:NOPE + hr], ropeA[:, :, 0, 0:hr], ropeB[:, :, 0, hr:ROPE], ALU.subtract))
                    c.step(tt(ktok[:, :, h, NOPE + hr:QKD], ropeB[:, :, 0, 0:hr], ropeA[:, :, 0, hr:ROPE], ALU.add))
                b = ring.take()
                ring.free(V.tensor_scalar(ckvT, b[:, :], col[:, C_GKV:C_GKV + 1], None, ALU.mult))
                for t in range(T0, NT):
                    b = ring.take()
                    ring.free(V.tensor_copy(qtok[:, t, :, :], split(b[:, 0:HEADS * QKD], h=HEADS, n=QKD)))
                qr = qtok[:, T0:NT, :, NOPE:QKD]
                rshape = [P, n_out, HEADS, ROPE]
                rA_, rB_ = ropeA[:, T0:NT], ropeB[:, T0:NT]
                c.step(tt(rA_, qr, spread(cosA[:, T0:NT, :], rshape, 2), ALU.mult))
                c.step(tt(rB_, qr, spread(sinA[:, T0:NT, :], rshape, 2), ALU.mult))
                c.step(tt(qr[:, :, :, 0:hr], rA_[:, :, :, 0:hr], rB_[:, :, :, hr:ROPE], ALU.subtract))
                c.step(tt(qr[:, :, :, hr:ROPE], rB_[:, :, :, 0:hr], rA_[:, :, :, hr:ROPE], ALU.add))
                c.await_("mla_keys")
                c.tell("mla_rotated")
                for h in range(HEADS):
                    b = ring.take()
                    ring.free(V.tensor_scalar(qT[0:QKD, h, T0 * P:TOK], b[0:QKD, T0 * P:TOK], QKD ** -0.5, None, ALU.mult))
                units = [(t, h) for t in range(T0, NT) for h in range(HEADS)]
                ub = 16 * L

                def row_max(i):
                    nk = CTX if units[i][0] < 2 else TOK
                    dve.wait_ge(S("scores_filled"), ub + i + 1)
                    V.tensor_reduce(small[:, 64 + i:65 + i], bank[i % 2][:, 0:nk], AX.X, ALU.max, negate=True
                                    ).then_inc(S("row_max"), 1)

                row_max(0)
                row_max(1)
                for i, (t, h) in enumerate(units):
                    nk = CTX if t < 2 else TOK
                    dve.wait_ge(S("turned_filled"), ub + i + 1)
                    if i >= 2:
                        dve.wait_ge(S("weighed"), ub + i - 1)
                    V.tensor_copy(pT[:, i % 2, 0:nk], bank[2 + i % 2][:, 0:nk]).then_inc(S("turned_emptied"), 1)
                    if i + 2 < len(units):
                        row_max(i + 2)
                    if h == HEADS - 1:
                        n = i // HEADS
                        inv = small[:, 104:108]
                        dve.wait_ge(S("probs_ready"), ub + i + 1)
                        c.step(V.reciprocal(inv, small[:, 48 + i - 3:49 + i]))
                        dve.wait_ge(S("weighed"), ub + i + 1)
                        tt(split(ptok[:, t, O_CQ:O_CQ + GW], h=HEADS, n=VD), split(bank[4 + n % 2][:, 0:GW], h=HEADS, n=VD),
                           spread(inv, [P, HEADS, VD], 2), ALU.mult).then_inc(S("tile_attended"), 1)
                        dve.wait_ge(S("tile_attended"), ub // HEADS + n + 1)

                b = ring.take()
                ring.free(V.tensor_copy(lrT[0:32, :], b[0:32, :]))
                c.await_("gla_logs")
                c.step(V.scalar_tensor_tensor(gz, gz, 0.0, ge, ALU.min, ALU.subtract))
                gcv = split(gc, d=2, t=NT, i=P)
                gzv = split(gz, d=2, t=NT, i=P)
                for t in range(NT):
                    c.step(V.tensor_tensor_scan(gcv[:, 0, t, :], C("ones"), gzv[:, 0, t, :], 0.0, ALU.mult, ALU.add))
                    c.step(V.tensor_tensor_scan(gcv[:, 1, t, ::-1], C("ones"), gzv[:, 1, t, ::-1], 0.0, ALU.mult, ALU.add))
                gs = split(small[:, 112:136], w=3, d=2, t=NT)
                for d in range(2):
                    c.step(V.tensor_copy(gs[:, 0, d, :], gcv[:, d, :, P // 2 - 1 + d]))
                    c.step(V.tensor_copy(gs[:, 1, d, :], gcv[:, d, :, P - 1 if d == 0 else 0]))
                c.step(tt(gs[:, 2], gs[:, 1], gs[:, 0], ALU.subtract))
                c.step(tt(split(ge, w=8, i=P), split(gc, w=8, i=P), spread(small[:, 112:120], [P, 8, P], 2), ALU.subtract))
                c.tell("gla_cums")
                c.await_("gla_exps")
                c.step(tt(split(gE1, d=2, t=TOK), split(gE1, d=2, t=TOK), spread(gqT, [P, 2, TOK], 1), ALU.mult))
                c.step(tt(split(gE2, d=2, t=TOK), split(gE2, d=2, t=TOK), spread(gkT, [P, 2, TOK], 1), ALU.mult))
                c.tell("gla_scaled")
                for st in range(NT - 1):
                    for d in range(2):
                        t, nxt = ORDER[d][st], ORDER[d][st + 1]
                        b = ring.take()
                        s_now, tmp = work[:, d, :], work[:, 2 + d, :]
                        ring.free(V.scalar_tensor_tensor(s_now if st == 0 else tmp, b[:, 0:GW], gs[:, 2, d, t:t + 1], C("blockdiag"),
                                                         ALU.mult, ALU.mult))
                        if st:
                            c.step(V.scalar_tensor_tensor(s_now, s_now, gs[:, 1, d, t:t + 1], tmp, ALU.mult, ALU.add))
                        c.step(V.tensor_scalar(states[:, d, nxt, :], s_now, gs[:, 0, d, nxt:nxt + 1], None, ALU.mult))
                c.tell("states_ready")
                hshape = [P, HEADS, P]
                for n, t in enumerate(range(T0, NT)):
                    for d in range(2):
                        c.step(tt(gQx[:, d, :, :], spread(gE1[:, d * TOK + t * P:d * TOK + (t + 1) * P], hshape, 1),
                                  spread(C("headmask"), hshape, 2), ALU.mult))
                        c.tell("gla_spread")
                    for d, mask in enumerate(("maskF", "maskB")):
                        b = ring.take()
                        ring.free(tt(split(mats[:, n % 2, d, :], h=HEADS, i=P), split(b[:, :], h=HEADS, i=P),
                                     spread(C(mask), hshape, 1), ALU.mult))
                c.await_("gla_outs")
                head_scale(O_GQ, T0, False, row[:, R_GLA:R_GLA + GW], O_GR, "gla_meansq")

                qk = ptok[:, :, O_RQ:O_RQ + 256].rearrange("p t (h n) -> p t h n", n=DK)
                for o, tab in ((rA, "cosR"), (rB, "sinR")):
                    c.step(tt(o, qk, spread(split(C(tab), t=NT, n=DK), [P, NT, 8, DK], 2), ALU.mult))
                c.step(tt(qk[:, :, :, 0:16], rA[:, :, :, 0:16], rB[:, :, :, 16:32], ALU.subtract))
                c.step(tt(qk[:, :, :, 16:32], rB[:, :, :, 0:16], rA[:, :, :, 16:32], ALU.add))
                c.tell("ret_rotated")
                for d, w in enumerate(("retWF", "retWB")):
                    for t in range(NT):
                        c.step(tt(split(rV[:, d, t, :], h=HEADS, v=DV), split(ptok[:, t, O_RV:O_RV + GW], h=HEADS, v=DV),
                                  spread(C(w), [P, HEADS, DV], 2), ALU.mult))
                c.await_("ret_turned")
                for d, w in enumerate(("retQF", "retQB")):
                    c.step(tt(rQ[:, d], rqT, spread(C(w), [P, NT, P], 1), ALU.mult))
                c.tell("ret_scaled")
                for st in range(NT - 1):
                    for d in range(2):
                        t, nxt = ORDER[d][st], ORDER[d][st + 1]
                        b = ring.take()
                        o = states[:, d, nxt, :] if st == 0 else work[:, d, :]
                        ring.free(tt(o, b[:, 0:GW], C("blockdiag"), ALU.mult))
                        if st:
                            c.step(V.scalar_tensor_tensor(states[:, d, nxt, :], states[:, d, t, :], C("retDec"), o, ALU.mult, ALU.add))
                c.tell("states_ready")
                for n, t in enumerate(range(T0, NT)):
                    c.step(tt(rQx[:, n % 2], spread(rqT[:, t, :], hshape, 1), spread(C("headmask"), hshape, 2), ALU.mult))
                    c.tell("ret_spread")
                    b = ring.take()
                    ring.free(tt(mats[:, n % 2, 0, :], b[:, :], C("retD"), ALU.mult))
                c.await_("ret_outs")
                head_scale(O_RQ, T0, True, None, O_RG, "ret_meansq")

                tshape = [P, NT, 8]
                c.step(tt(s_dt, ptok[:, :, O_DT:O_DT + 8], spread(row[:, R_DTB:R_DTB + 8], tshape, 1), ALU.add))
                c.tell("ssd_rates_raw")
                c.await_("ssd_logs")
                c.step(V.scalar_tensor_tensor(s_dt, s_dt, 0.0, s_t, ALU.max, ALU.add))
                c.step(V.scalar_tensor_tensor(s_la, s_dt, -1.0, spread(small[:, 136:144], tshape, 1), ALU.mult, ALU.mult))
                c.tell("ssd_rates")
                b = ring.take()
                ring.free(V.tensor_copy(s_cum, split(b[:, 0:32], t=NT, n=8)))
                b = ring.take()
                ring.free(V.tensor_copy(s_t, split(b[:, 0:32], t=NT, n=8)))
                c.step(tt(s_w, s_t, s_cum, ALU.subtract))
                c.tell("ssd_sums")
                c.await_("ssd_decays")
                c.step(tt(s_w, s_w, s_dt, ALU.mult))
                vshape = [P, NT, HEADS, DV]
                xh = xBtok[:, :, 0:GW].rearrange("p t (h v) -> p t h v", h=HEADS)
                for d in range(2):
                    for o, w in ((sV, s_dt), (sVw, s_w)):
                        c.step(tt(o[:, d].rearrange("p t (h v) -> p t h v", h=HEADS), xh,
                                  spread(w[:, :, 4 * d:4 * d + 4], vshape, 3), ALU.mult))
                c.tell("ssd_values")
                for st in range(NT - 1):
                    for d in range(2):
                        t, nxt = ORDER[d][st], ORDER[d][st + 1]
                        b = ring.take()
                        if st == 0:
                            ring.free(V.tensor_copy(states[:, d, nxt, :], b[:, 0:GW]))
                        else:
                            c.step(tt(split(states[:, d, nxt, :], h=HEADS, v=DV), split(states[:, d, t, :], h=HEADS, v=DV),
                                      spread(s_el[:, t, 4 * d:4 * d + 4], [P, HEADS, DV], 2), ALU.mult))
                            ring.free(tt(states[:, d, nxt, :], states[:, d, nxt, :], b[:, 0:GW], ALU.add))
                c.tell("states_ready")
                for t in range(T0, NT):
                    for d, mask in enumerate(("maskF", "maskB")):
                        c.step(tt(laM[:, d], spread(C(mask), hshape, 1), spread(s_la[:, t, 4 * d:4 * d + 4], hshape, 2), ALU.mult))
                        c.tell("ssd_masked")
                    for d, neg in enumerate(("negF", "negB")):
                        b = ring.take()
                        ring.free(V.tensor_copy(sE[:, d], split(b[:, :], h=HEADS, i=P)))
                        c.step(tt(sD[:, d], sE[:, d], spread(s_cum[:, t, 4 * d:4 * d + 4], hshape, 2), ALU.subtract))
                        c.step(tt(sD[:, d], sD[:, d], spread(C(neg), hshape, 1), ALU.add))
                    c.tell("ssd_exponents")
                    c.await_("ssd_exps")
                    gshape = [P, 2, 2, P]
                    b = ring.take()
                    for d in range(2):
                        c.step(tt(sQ[:, d].rearrange("p (g e) i -> p g e i", g=2), spread(cvT[:, 4:6, t * P:(t + 1) * P], gshape, 2),
                                  sE[:, d].rearrange("p (g e) i -> p g e i", g=2), ALU.mult))
                    for d in range(2):
                        ins = tt(split(sM[:, d, :], g=2, e=2, i=P), spread(split(b[:, 0:256], g=2, i=P), gshape, 2),
                                 sD[:, d].rearrange("p (g e) i -> p g e i", g=2), ALU.mult)
                        if d == 0:
                            c.step(ins)
                        else:
                            ring.free(ins)
                    c.tell("ssd_decayed")
                c.await_("ssd_outs")
                xh = xBtok[:, T0:NT, 0:GW].rearrange("p t (h v) -> p t h v", h=HEADS)
                vshape = [P, n_out, HEADS, DV]
                dsk = row[:, R_DSK:R_DSK + HEADS].unsqueeze(1).unsqueeze(3).to_broadcast(vshape)
                y = xBtok[:, T0:NT, 0:GW]
                zc = ptok[:, T0:NT, O_Z:O_Z + GW]
                c.step(tt(xh, xh, dsk, ALU.mult))
                c.step(tt(y, y, sVw[:, 0, T0:NT, :], ALU.add))
                c.step(tt(zc, zc, y, ALU.mult))
                c.step(tt(norm_sq[:, T0:NT, :], zc, zc, ALU.mult))
                if T0:
                    c.step(V.memset(small[:, 80:84], 1.0))
                c.step(V.tensor_reduce(small[:, 80:80 + n_out], norm_sq[:, T0:NT, :], AX.X, ALU.add))
                c.step(V.tensor_scalar(small[:, 80:84], small[:, 80:84], 1.0 / GW, 1e-6, ALU.mult, ALU.add))
                c.tell("ssd_meansq")
                c.await_("ssd_meansq_root")
                refined(small[:, 80:84], small[:, 96:100], 4)
                c.step(tt(zc, zc, spread(small[:, 96:96 + n_out], [P, n_out, GW], 2), ALU.mult))
                c.step(tt(zc, zc, spread(row[:, R_SSD:R_SSD + GW], [P, n_out, GW], 1), ALU.mult))
                c.tell("mixed")
                for k in range(1, KD, 2):
                    b = ring.take()
                    ring.free(V.tensor_copy(xmT[:, k, T0 * P:TOK], b[:, T0 * P:TOK]))
                tiles = list(range(T0, NT))
                if T0:
                    c.step(V.memset(small[:, 132:136], 1.0))
                layer_norm(lambda t: X[:, t, :], tiles, scratch(W2, 512), [(t, hf) for hf in range(2) for t in tiles],
                           lambda t: lnr[:, 2 + t // 2, :], lambda r: lnr[:, r, :])

            def experts(s, L, g):
                for k in range(1, KD, 2):
                    b = ring.take()
                    modulated(xTk[:, k, :], b, k, g, 0, 256, 3, True)
                c.tell("x_modulated")
                dve.wait_ge(S("x_high"), s + 1)
                tt(xTr[:, 1, :, :], xTk, xTr[:, 0, :, :].bitcast(F32), ALU.subtract).then_inc(S("x_split"), 1)

                def top16(vals_, idx_, src, spare, release):
                    c.step(V.max(vals_[:, 0:8], src))
                    c.step(V.max_index(idx_[:, 0:8], vals_[:, 0:8], src))
                    ins = V.match_replace(spare, vals_[:, 0:8], src, -3.0e38)
                    if release:
                        ring.free(ins)
                    else:
                        c.step(ins)
                    c.step(V.max(vals_[:, 8:16], spare))
                    c.step(V.max_index(idx_[:, 8:16], vals_[:, 8:16], spare))

                for bl in range(2 * PH):
                    b = ring.take()
                    for t in range(2):
                        top16(vals[:, t, bl, :], idxu[:, t, bl, :], b[:, t * P:(t + 1) * P], ctmp[:, 0:P], t == 1)
                    dve.sem_inc(S("query_used"), 1)
                c.step(V.tensor_copy(idxf, idxu))
                cshape = [P, PH, 16, 16]
                for t in range(2):
                    v4 = vals[:, t].rearrange("p (h w) n -> p h w n", w=2)
                    c.step(tt(cand.rearrange("p h (a b) -> p h a b", a=16), spread(v4[:, :, 0, :], cshape, 3),
                              spread(v4[:, :, 1, :], cshape, 2), ALU.add))
                    for h in range(PH):
                        top16(vsel[:, t, h, :], cidxu[:, t, h, :], cand[:, h, :], ctmp, False)
                sshape = [P, 2, PH, 16]
                c.step(V.tensor_copy(small[:, 112:128], vsel[:, :, :, 0].rearrange("p t h -> p (t h)"))
                       if False else V.tensor_copy(split(small[:, 112:128], t=2, h=PH), vsel[:, :, :, 0]))
                c.step(tt(vsel, vsel, spread(split(small[:, 112:128], t=2, h=PH), sshape, 3), ALU.subtract))
                c.tell("softmax_shifted")
                c.step(V.tensor_scalar(cab[:, 0:256], cidx, 4, None, ALU.logical_shift_right))
                c.step(V.tensor_scalar(cab[:, 256:512], cidx, 15, None, ALU.bitwise_and))
                c.step(V.tensor_copy(cabf, cab))
                cab5 = split(cabf, w=2, t=2, h=PH, k=16)
                i16 = iota[:, 0:16].unsqueeze(1).unsqueeze(1).to_broadcast([P, PH, 16, 16])
                for t in range(2):
                    i4 = idxf[:, t].rearrange("p (h w) n -> p h w n", w=2)
                    for w in range(2):
                        c.step(tt(eq, spread(cab5[:, w, t], cshape, 3), i16, ALU.is_equal))
                        c.step(tt(eq, eq, spread(i4[:, :, w, :], cshape, 2), ALU.mult))
                        c.step(V.tensor_reduce(split(sel[:, w, t, :], h=PH, k=16), eq, AX.X, ALU.add))
                c.await_("softmax_exps")
                c.step(V.tensor_reduce(split(small[:, 112:128], t=2, h=PH), vsel, AX.X, ALU.add))
                c.step(V.reciprocal(small[:, 128:144], small[:, 112:128]))
                c.step(tt(sel[:, 2].rearrange("p t (h k) -> p t h k", h=PH), vsel,
                          spread(split(small[:, 128:144], t=2, h=PH), sshape, 3), ALU.mult))
                c.tell("picked")
                for w in range(3):
                    b = ring.take()
                    ring.free(V.tensor_copy(picks[:, w, :], b[:, 0:256]))
                base = BLOCKS * s

                def low(name, n, sl, w):
                    dve.wait_ge(S(f"{name}_high"), base + n + 1)
                    tt(splits[:, 2 * w + sl, 1, :], raw[:, w, sl, :], splits[:, 2 * w + sl, 0, :].bitcast(F32),
                       ALU.subtract).then_inc(S(f"{name}_split"), 1)

                low("u", 0, 0, 0)
                low("u", 1, 1, 0)
                low("v", 0, 0, 1)
                gb = 64 * s

                def hots(i, u):
                    n = gb + 4 * i + u
                    if not isinstance(n, int) or n >= 2:
                        dve.wait_ge(S("gates_filled"), n - 1)
                    for q in range(4):
                        at = (16 * i + 4 * u + q)
                        V.tensor_scalar(hotJ[:, u % 2, q, :], iota[:, :], picks[:, 1, bass.ds(at, 1)], None, ALU.is_equal)
                        ins = V.tensor_scalar(hotI[:, u % 2, q, :], iota[:, :], picks[:, 0, bass.ds(at, 1)],
                                              picks[:, 2, bass.ds(at, 1)], ALU.is_equal, ALU.mult)
                    ins.then_inc(S("hots_ready"), 1)

                for u in range(4):
                    hots(0, u)
                with dve.Fori(1, 16) as i:
                    for u in range(4):
                        hots(i, u)
                dve.wait_ge(S("gates_emptied"), gb + 64)

                def block_work(n, sl, more_u, more_v):
                    dve.wait_ge(S("gelu_done"), base + n + 1)
                    tt(acts[:, sl, :], acts[:, sl, :], gates[:, :, bass.ds(n, 1)].rearrange("p t o -> p (t o)"),
                       ALU.mult).then_inc(S("act_weighed"), 1)
                    dve.wait_ge(S("act_high"), base + n + 1)
                    tt(actr[:, sl, 1, :], acts[:, sl, :], actr[:, sl, 0, :].bitcast(F32), ALU.subtract).then_inc(S("act_ready"), 1)
                    if more_u:
                        low("u", n + 2, sl, 0)
                    if more_v:
                        low("v", n + 1, 1 - sl, 1)

                with dve.Fori(0, BLOCKS // 2 - 1) as i:
                    block_work(2 * i, 0, True, True)
                    block_work(2 * i + 1, 1, True, True)
                block_work(BLOCKS - 2, 0, False, True)
                block_work(BLOCKS - 1, 1, False, False)
                dve.wait_ge(S("rows_in"), 16 * 4 * (s + 1))
                c.step(V.memset(small[:, 132:136], 1.0))
                layer_norm(lambda t: xs3[:, t, :], [0, 1], scratch(5120, 512), [(t, hf) for t in range(2) for hf in range(2)],
                           lambda t: grow[:, 0, :], lambda r: grow[:, 1 + r, :])

            s = 0
            for L in range(DEPTH):
                mixers(L)
                while s < len(SWEEPS) and SWEEPS[s][0] == L:
                    experts(s, *SWEEPS[s])
                    s += 1


def shape_constants():
    f = np.float32
    out = np.zeros((P, NCONST), f)

    def put(name, a):
        at, n = CONST[name]
        out[:, at:at + n] = np.asarray(a, f).reshape(P, n)

    j, i = np.arange(P)[:, None], np.arange(P)[None, :]
    put("maskF", j <= i)
    put("maskB", j >= i)
    put("negF", np.where(j <= i, 0.0, -1e30))
    put("negB", np.where(j >= i, 0.0, -1e30))
    log_decay = np.log1p(-np.exp2(-5.0 - np.arange(HEADS)))
    power = np.exp(np.abs(i - j)[:, None, :] * log_decay[None, :, None])
    put("retD", power * (1 + (i == j))[:, None, :])
    by_row = np.repeat(log_decay, DK)[:, None]
    put("retQF", np.exp(by_row * (i + 1)))
    put("retQB", np.exp(by_row * (P - i)))
    put("retWF", np.exp(log_decay[None] * (P - 1 - j)))
    put("retWB", np.exp(log_decay[None] * j))
    put("retDec", np.exp(by_row * P))
    head_of_row, head_of_col = np.arange(P)[:, None] // DK, np.arange(GW)[None] // DV
    put("blockdiag", head_of_row == head_of_col)
    put("headmask", head_of_row == np.arange(HEADS)[None])
    put("ones", np.ones((P, P)))

    def table(pos, half):
        freq = (10000.0 ** (-np.arange(half, dtype=f) / f(half))).astype(f)
        ang = pos.astype(f)[:, None] * freq
        return np.cos(ang.astype(np.float64)), np.sin(ang.astype(np.float64))

    n = np.arange(SEQ)
    crow, srow = table(n // GRID_W, ROPE // 4)
    ccol, scol = table(n % GRID_W, ROPE // 4)
    cr, sr = table(n, DK // 2)
    for name, c, rest in (("cosA", np.concatenate([crow, ccol] * 2, 1), 1.0), ("sinA", np.concatenate([srow, scol] * 2, 1), 0.0),
                          ("cosR", np.concatenate([cr] * 2, 1), 1.0), ("sinR", np.concatenate([sr] * 2, 1), 0.0)):
        full = np.concatenate([np.full((CTX, c.shape[1]), rest), c], 0)
        put(name, full.reshape(NT, P, -1).transpose(1, 0, 2))
    return out


def lay_out(a):
    def chunks(w, n):
        L = w.shape[0]
        return np.ascontiguousarray(w.reshape(L, KD, P, n, 512).transpose(0, 3, 2, 1, 4)).reshape(L * n, P, CHUNK)

    L = DEPTH
    rope = np.concatenate([np.arange(0, 8), np.arange(16, 24), np.arange(8, 16), np.arange(24, 32)])
    order = np.concatenate([np.arange(1472, 2240), np.arange(0, 384), 384 + rope, np.arange(416, 1472),
                            np.arange(2240, 3016)])
    win = np.concatenate([a["w_in"][:, :, order], np.zeros((L, D, NWIN * 512 - order.size), np.float32)], 2)
    uq_order = np.concatenate([np.concatenate([np.arange(NOPE), NOPE + rope]) + QKD * h for h in range(HEADS)])
    uq = a["mla_w_uq"][:, :, uq_order].reshape(L, 2, P, HEADS * QKD).transpose(0, 2, 1, 3).reshape(L, P, -1)
    gate_w = np.zeros((L, P, 2, P), np.float32)
    gate_w[:, 0:RANK, 0] = a["gla_w_gf"]
    gate_w[:, RANK:2 * RANK, 1] = a["gla_w_gb"]
    smallw = np.concatenate([uq, a["mla_w_uk"], a["mla_w_uv"], gate_w.reshape(L, P, 2 * P)], 2)
    col = np.zeros((L, P, NCOL), np.float32)
    col[:, :, C_GQ:C_GQ + 2] = a["mla_g_q"].reshape(L, 2, P).transpose(0, 2, 1)
    col[:, :, C_GKV] = a["mla_g_kv"]
    col[:, :, C_BGF], col[:, :, C_BGB] = a["gla_b_gf"], a["gla_b_gb"]
    col[:, :, C_CW:C_CB] = a["ssd_conv_w"].reshape(L, 3, NXB, P).transpose(0, 3, 2, 1).reshape(L, P, 3 * NXB)
    col[:, :, C_CB:] = a["ssd_conv_b"].reshape(L, NXB, P).transpose(0, 2, 1)
    rows = np.concatenate([a[k] for k in ("gla_g", "ssd_g", "ssd_dt_bias_f", "ssd_dt_bias_b", "ssd_a_log_f", "ssd_a_log_b", "ssd_d")], 1)
    u = a["peer_u"].reshape(L * BLOCKS, P, KD, P).transpose(0, 3, 2, 1)
    return {
        "x": a["x"], "ctx": a["ctx"],
        "c_cols": a["c"].reshape(KD, P).T, "cctx_cols": a["c_ctx"].reshape(KD, P).T,
        "wada": chunks(a["w_ada"], NADA), "b_ada": a["b_ada"], "win": chunks(win, NWIN), "wout": chunks(a["w_out"], NWOUT),
        "wq": chunks(a["peer_w_q"], NWQ), "u": u.reshape(L * BLOCKS, P, D), "v": a["peer_v"].reshape(L * BLOCKS, P, D),
        "smallw": smallw, "cols": col, "rows": rows, "keys": a["peer_keys"].transpose(0, 3, 1, 2),
        "ln": np.stack([a[k] for k in ("ln1_g", "ln1_b", "ln2_g", "ln2_b")], 1),
        "const": shape_constants(), "ident": np.eye(P, dtype=np.float32),
        "iota": np.tile(np.arange(P, dtype=np.float32), (P, 1)),
    }


def kernel(**inputs):
    import concourse.bacc as _bacc
    from concourse.bass_utils import run_bass_kernel_spmd as _run

    nc = _bacc.Bacc("TRN2", target_bir_lowering=False, num_devices=1)
    arrays, args = {}, {}
    for name, value in lay_out({k: np.asarray(v) for k, v in inputs.items()}).items():
        value = np.ascontiguousarray(value)
        arrays[f"in_{name}_dram"] = value
        args[name] = nc.dram_tensor(f"in_{name}_dram", value.shape, mybir.dt.from_np(value.dtype), kind="ExternalInput").ap()
    out = nc.dram_tensor("out_0_dram", (1, SEQ, D), F32, kind="ExternalOutput").ap()
    build(nc, args, out)
    r = _run(nc, [arrays], core_ids=[0])
    return r.results[0]["out_0_dram"]
```
